# Optimizing a Trainium2 kernel written in Bass

```python
import math
import jax, jax.numpy as jnp
from jax import lax
import numpy as np

D_MODEL = 2048
BATCH = 1
SEQ = 256
DEPTH = 1

D_MIX = D_MODEL
D_ATTN = D_MIX // 2
D_SSM = D_MIX - D_ATTN
QK_HEAD_DIM = 64
V_HEAD_DIM = 2 * QK_HEAD_DIM
N_ATTN_HEADS = D_ATTN // V_HEAD_DIM
D_QK = 2 * N_ATTN_HEADS * QK_HEAD_DIM
SSM_GROUP = 16
N_SSM_GROUPS = D_SSM // SSM_GROUP
SSM_STATE = 64
D_IN = 2 * D_QK + D_ATTN + D_SSM
D_FF = ((8 * D_MODEL // 3) + 255) // 256 * 256
CONV_WIDTH = 3
N_BUCKETS = 32
MAX_DISTANCE = 128
Q_BLOCK = 128
EPS = 1e-6
DT_MIN = 1e-3
DT_MAX = 1e-1

kernel_name = "hymba_style_diffattn_s5_convffn_layer"

def rms_norm(x, g):
    xf = x.astype(jnp.float32)
    y = xf * lax.rsqrt(jnp.mean(xf * xf, axis=-1, keepdims=True) + EPS)
    return (y * g.astype(jnp.float32)).astype(x.dtype)

def t5_causal_bucket(dist):
    n = jnp.maximum(dist, 0)
    max_exact = N_BUCKETS // 2
    nf = jnp.maximum(n, 1).astype(jnp.float32)
    large = max_exact + (jnp.log(nf / max_exact) / math.log(MAX_DISTANCE / max_exact)
                         * (N_BUCKETS - max_exact)).astype(jnp.int32)
    large = jnp.minimum(large, N_BUCKETS - 1)
    return jnp.where(n < max_exact, n, large)

def diff_attention(q, k, v, rel_bias, lam_q1, lam_k1, lam_q2, lam_k2, sub_norm, lambda_init):
    B, S = q.shape[0], q.shape[1]
    H = N_ATTN_HEADS
    nb = S // Q_BLOCK
    lam = (jnp.exp(jnp.sum(lam_q1.astype(jnp.float32) * lam_k1.astype(jnp.float32)))
           - jnp.exp(jnp.sum(lam_q2.astype(jnp.float32) * lam_k2.astype(jnp.float32)))
           + lambda_init)
    k_pos = jnp.arange(S, dtype=jnp.int32)
    q_blocks = (q * (QK_HEAD_DIM ** -0.5)).reshape(B, nb, Q_BLOCK, 2 * H, QK_HEAD_DIM)
    q_blocks = q_blocks.transpose(1, 0, 2, 3, 4)

    def one_block(args):
        qb, i = args
        q_pos = i * Q_BLOCK + jnp.arange(Q_BLOCK, dtype=jnp.int32)
        dist = q_pos[:, None] - k_pos[None, :]
        bias = jnp.transpose(rel_bias[t5_causal_bucket(dist)], (2, 0, 1))
        s = jnp.einsum('bqhd,bkhd->bhqk', qb, k).astype(jnp.float32)
        s = s.reshape(B, H, 2, Q_BLOCK, S) + bias[None, :, None].astype(jnp.float32)
        s = jnp.where(dist >= 0, s, -jnp.inf)
        p = jax.nn.softmax(s, axis=-1)
        a = p[:, :, 0] - lam * p[:, :, 1]
        return jnp.einsum('bhqk,bkhd->bqhd', a.astype(v.dtype), v)

    out = lax.map(one_block, (q_blocks, jnp.arange(nb, dtype=jnp.int32)))
    out = out.transpose(1, 0, 2, 3, 4).reshape(B, S, H, V_HEAD_DIM)
    out = rms_norm(out, sub_norm) * (1.0 - lambda_init)
    return out.reshape(B, S, H * V_HEAD_DIM)

def _complex_affine_combine(e_i, e_j):
    ar_i, ai_i, br_i, bi_i = e_i
    ar_j, ai_j, br_j, bi_j = e_j
    ar = ar_j * ar_i - ai_j * ai_i
    ai = ar_j * ai_i + ai_j * ar_i
    br = ar_j * br_i - ai_j * bi_i + br_j
    bi = ar_j * bi_i + ai_j * br_i + bi_j
    return (ar, ai, br, bi)

def s5_mixer(u, a_re, a_im, log_dt, b_re, b_im, c_re, c_im, d_skip, w_glu):
    B, S = u.shape[0], u.shape[1]
    G, Hc, P = N_SSM_GROUPS, SSM_GROUP, SSM_STATE
    uf = u.astype(jnp.float32).reshape(B, S, G, Hc)
    dt = jnp.exp(log_dt.astype(jnp.float32))[:, None]
    ar = a_re.astype(jnp.float32)
    ai = a_im.astype(jnp.float32)
    mag = jnp.exp(ar * dt)
    lb_re = mag * jnp.cos(ai * dt)
    lb_im = mag * jnp.sin(ai * dt)
    den = ar * ar + ai * ai
    nr, ni = lb_re - 1.0, lb_im
    f_re = (nr * ar + ni * ai) / den
    f_im = (ni * ar - nr * ai) / den
    br = b_re.astype(jnp.float32)
    bi = b_im.astype(jnp.float32)
    bb_re = f_re[..., None] * br - f_im[..., None] * bi
    bb_im = f_re[..., None] * bi + f_im[..., None] * br
    bu_re = jnp.einsum('bsgh,gph->bsgp', uf, bb_re)
    bu_im = jnp.einsum('bsgh,gph->bsgp', uf, bb_im)
    a_seq_re = jnp.broadcast_to(lb_re, (1, S, G, P))
    a_seq_im = jnp.broadcast_to(lb_im, (1, S, G, P))
    _, _, x_re, x_im = lax.associative_scan(
        _complex_affine_combine, (a_seq_re, a_seq_im, bu_re, bu_im), axis=1)
    y = (jnp.einsum('bsgp,ghp->bsgh', x_re, c_re.astype(jnp.float32))
         - jnp.einsum('bsgp,ghp->bsgh', x_im, c_im.astype(jnp.float32))
         + d_skip.astype(jnp.float32) * uf)
    y = jax.nn.gelu(y.reshape(B, S, D_SSM)).astype(u.dtype)
    z = y @ w_glu
    return z[..., :D_SSM] * jax.nn.sigmoid(z[..., D_SSM:])

def conv_ffn(x, w_up, conv_w, conv_b, w_down):
    h = x @ w_up
    h = lax.conv_general_dilated(h, conv_w.astype(h.dtype), window_strides=(1,),
                                 padding=[(CONV_WIDTH - 1, 0)],
                                 dimension_numbers=('NWC', 'WIO', 'NWC'),
                                 feature_group_count=2 * D_FF) + conv_b
    g, val = jnp.split(h, 2, axis=-1)
    return (jax.nn.silu(g) * val) @ w_down

def setup_inputs(seed: int = 0) -> dict:
    key = jax.random.key(seed)
    ks = jax.random.split(key, 26)
    nrm = lambda k, shape, s: jax.random.normal(k, shape, jnp.float32) * s
    L, G, P, Hc = DEPTH, N_SSM_GROUPS, SSM_STATE, SSM_GROUP
    n_idx = jnp.arange(P, dtype=jnp.float32)
    return {
        "x": nrm(ks[0], (BATCH, SEQ, D_MODEL), 1.0),
        "ln_pre_mix": 1.0 + nrm(ks[1], (L, D_MODEL), 0.02),
        "ln_post_mix": 1.0 + nrm(ks[2], (L, D_MODEL), 0.02),
        "ln_pre_ffn": 1.0 + nrm(ks[3], (L, D_MODEL), 0.02),
        "ln_post_ffn": 1.0 + nrm(ks[4], (L, D_MODEL), 0.02),
        "w_in": nrm(ks[5], (L, D_MODEL, D_IN), D_MODEL ** -0.5),
        "lam_q1": nrm(ks[6], (L, QK_HEAD_DIM), 0.1),
        "lam_k1": nrm(ks[7], (L, QK_HEAD_DIM), 0.1),
        "lam_q2": nrm(ks[8], (L, QK_HEAD_DIM), 0.1),
        "lam_k2": nrm(ks[9], (L, QK_HEAD_DIM), 0.1),
        "attn_sub_norm": 1.0 + nrm(ks[10], (L, V_HEAD_DIM), 0.02),
        "rel_bias": nrm(ks[11], (N_BUCKETS, N_ATTN_HEADS), 0.5),
        "ssm_a_re": -0.5 + nrm(ks[12], (L, G, P), 0.01),
        "ssm_a_im": math.pi * n_idx + nrm(ks[13], (L, G, P), 0.01),
        "ssm_log_dt": jax.random.uniform(ks[14], (L, G), jnp.float32,
                                         math.log(DT_MIN), math.log(DT_MAX)),
        "ssm_b_re": nrm(ks[15], (L, G, P, Hc), (2 * Hc) ** -0.5),
        "ssm_b_im": nrm(ks[16], (L, G, P, Hc), (2 * Hc) ** -0.5),
        "ssm_c_re": nrm(ks[17], (L, G, Hc, P), (2 * P) ** -0.5),
        "ssm_c_im": nrm(ks[18], (L, G, Hc, P), (2 * P) ** -0.5),
        "ssm_d": nrm(ks[19], (L, G, Hc), 1.0),
        "ssm_w_glu": nrm(ks[20], (L, D_SSM, 2 * D_SSM), D_SSM ** -0.5),
        "w_out": nrm(ks[21], (L, D_MIX, D_MODEL), D_MIX ** -0.5),
        "w_up": nrm(ks[22], (L, D_MODEL, 2 * D_FF), D_MODEL ** -0.5),
        "conv_w": nrm(ks[23], (L, CONV_WIDTH, 1, 2 * D_FF), CONV_WIDTH ** -0.5),
        "conv_b": nrm(ks[24], (L, 2 * D_FF), 0.02),
        "w_down": nrm(ks[25], (L, D_FF, D_MODEL), D_FF ** -0.5),
    }

def reference(x, ln_pre_mix, ln_post_mix, ln_pre_ffn, ln_post_ffn, w_in,
              lam_q1, lam_k1, lam_q2, lam_k2, attn_sub_norm, rel_bias,
              ssm_a_re, ssm_a_im, ssm_log_dt, ssm_b_re, ssm_b_im, ssm_c_re, ssm_c_im,
              ssm_d, ssm_w_glu, w_out, w_up, conv_w, conv_b, w_down):
    B, S, _ = x.shape
    H = N_ATTN_HEADS
    for l in range(DEPTH):
        lambda_init = 0.8 - 0.6 * math.exp(-0.3 * l)
        xn = rms_norm(x, ln_pre_mix[l])
        h = xn @ w_in[l]
        q = h[..., :D_QK].reshape(B, S, 2 * H, QK_HEAD_DIM)
        k = h[..., D_QK:2 * D_QK].reshape(B, S, 2 * H, QK_HEAD_DIM)
        v = h[..., 2 * D_QK:2 * D_QK + D_ATTN].reshape(B, S, H, V_HEAD_DIM)
        u = h[..., 2 * D_QK + D_ATTN:]
        attn_out = diff_attention(q, k, v, rel_bias, lam_q1[l], lam_k1[l], lam_q2[l],
                                  lam_k2[l], attn_sub_norm[l], lambda_init)
        ssm_out = s5_mixer(u, ssm_a_re[l], ssm_a_im[l], ssm_log_dt[l], ssm_b_re[l],
                           ssm_b_im[l], ssm_c_re[l], ssm_c_im[l], ssm_d[l], ssm_w_glu[l])
        mix = jnp.concatenate([attn_out, ssm_out.astype(attn_out.dtype)], axis=-1) @ w_out[l]
        x = x + rms_norm(mix, ln_post_mix[l])
        f = conv_ffn(rms_norm(x, ln_pre_ffn[l]), w_up[l], conv_w[l], conv_b[l], w_down[l])
        x = x + rms_norm(f, ln_post_ffn[l])
    return x


_drawn_inputs = setup_inputs


def setup_inputs(seed=0):
    import zlib

    import numpy as np

    out = dict(_drawn_inputs(seed))
    spreads = {}
    factors = {'ln_post_mix': 3.376,
     'ln_pre_ffn': 3.549,
     'ln_post_ffn': 17.308,
     'lam_q1': 2.789,
     'lam_k2': 8.0,
     'attn_sub_norm': 3.286,
     'ssm_a_re': 64.0,
     'ssm_a_im': 24.144,
     'ssm_log_dt': 24.936,
     'ssm_b_re': 34.256,
     'ssm_b_im': 33.832,
     'ssm_c_re': 34.432,
     'ssm_c_im': 33.848,
     'conv_b': 3.431}
    for name, (base, spread) in spreads.items():
        noise = np.random.default_rng([zlib.crc32(name.encode()), seed]).standard_normal(out[name].shape)
        drawn = base * np.exp(spread * noise) if base else spread * noise
        out[name] = __import__('jax').numpy.asarray(drawn.astype(out[name].dtype))
    for name, factor in factors.items():
        out[name] = (out[name] * factor).astype(out[name].dtype)
    return out
```

```python
import math
from contextlib import ExitStack

import concourse.bass as bass
from concourse import mybir

F32 = mybir.dt.float32
F32R = mybir.dt.float32r
ALU = mybir.AluOpType
ACT = mybir.ActivationFunctionType
AX = mybir.AxisListType

P = 128
D = 2048
T = 256
TT = T // P
KT = D // P
D_SSM = D // 2
HEADS = 8
DH = 64
G, HC, PS = 64, 16, 64
NT = G // 2
UT = D_SSM // P
DFF = 5632
CH = 512
CK = 4
CHUNK = CK * CH
UNITS_FFN = DFF // CH
FT = DFF // P
EPS = 1e-6
NB = 32
BAND = T + P
LAMBDA_INIT = 0.8 - 0.6 * math.exp(-0.3 * 0)
NEG = -1e30

C_QKV, C_GLU, C_OUT, C_UP = 8, 32, 40, 56
S_GLU, S_OUT, S_UP, S_DOWN = 8, 16, 32, 120
RING = 4
N_QKV = C_GLU - C_QKV

MAGIC = 1.5 * 2 ** 23
MAGIC16 = 1.5 * 2 ** 7
INV2PI = 1.0 / (2 * math.pi)
PI_A = 6.28125
PI_B = math.floor((2 * math.pi - PI_A) * 2 ** 19) / 2 ** 19
PI_C = 2 * math.pi - PI_A - PI_B
PI_IN = 3.1415925
HALF_IN = 0.49999997


class Tally:

    def __init__(self, sem):
        self.sem, self.n = sem, 0

    def add(self, ins):
        ins.then_inc(self.sem, 1)
        self.n += 1
        return self.n


def build(nc, x, ln_pre_mix, ln_post_mix, ln_pre_ffn, ln_post_ffn, w_in, lam_q1, lam_k1, lam_q2, lam_k2,
          attn_sub_norm, rel_bias, ssm_a_re, ssm_a_im, ssm_log_dt, ssm_b_re, ssm_b_im, ssm_c_re, ssm_c_im,
          ssm_d, ssm_w_glu, w_out, w_up, conv_w, conv_b, w_down, bucket_onehot, out):
    band_dram = nc.dram_tensor("band_scratch", (HEADS, P, BAND), F32, kind="Internal").ap()

    with ExitStack() as ctx:
        def sb(name, shape, dt=F32):
            return ctx.enter_context(nc.sbuf_tensor(name, shape, dt))

        def sem(name):
            return ctx.enter_context(nc.semaphore(name))

        raw = sb("raw", [P, RING, CHUNK])
        w_hi = sb("w_hi", [P, RING, CHUNK], F32R)
        w_lo = sb("w_lo", [P, RING, CHUNK], F32R)
        xs = sb("xs", [P, KT, 2, T], F32R)
        res = sb("res", [P, TT * D])
        arena = sb("arena", [P, 17408])
        ident = sb("ident", [P, P])
        steps = sb("steps", [P, T])
        consts = sb("consts", [P, 2])
        ones = sb("ones", [1, P])
        prm = sb("prm", [P, P])
        prm2 = sb("prm2", [P, UT + 1])
        conv = sb("conv", [P, 4, 2 * FT])
        stat = sb("stat", [P, 4, 3, TT])
        heads_stat = sb("heads_stat", [P, 3, HEADS * TT])
        sm = sb("sm", [P, 2, 5, 2, 2])
        ssmp = sb("ssmp", [P, 20, NT])
        lamt = sb("lamt", [1, 4, DH])
        lamj = sb("lamj", [1, DH])
        lams = sb("lams", [1, 6])
        lam_col = sb("lam_col", [P, 1])
        gain_o = sb("gain_o", [P, 1])
        ps = ctx.enter_context(nc.psum_tensor("ps", [P, 8, 512], F32))

        def area(a, n):
            return arena[:, a:a + n]

        x_nat = area(0, 4096).rearrange("p (t d) -> p t d", t=TT)
        qT = area(0, 2048).rearrange("p (m t) -> p m t", t=T)
        kT = area(2048, 2048).rearrange("p (m t) -> p m t", t=T)
        v = area(4096, 2048).rearrange("p (t d) -> p t d", t=TT)
        uT = area(6144, 2048).rearrange("p (m t) -> p m t", t=T)
        zT = uT
        BT = [area(8192 + 1024 * a, 1024).rearrange("p (j q) -> p j q", j=UT) for a in (0, 1)]
        CS = [area(10240 + 1024 * a, 1024).rearrange("p (i e h) -> p i e h", i=NT, e=2) for a in (0, 1)]
        band = area(8192, 3072).rearrange("p (h c) -> p h c", h=HEADS)
        onehot = arena[0:NB + 1, 8192:8192 + BAND]
        bandrow = arena[0:HEADS, 8576:8576 + BAND]
        relb = arena[0:NB + 1, 8960:8960 + HEADS]
        b_diag = [area(4096 + 1024 * a, 1024).rearrange("p (i e h) -> p i e h", i=NT, e=2) for a in (0, 1)]
        c_nat = [area(6144 + 1024 * a, 1024).rearrange("p (j e q) -> p j e q", j=UT, e=2) for a in (0, 1)]
        TMP = 12288
        junk = area(TMP, 2048)
        b_nat = [area(TMP + 2048 + 512 * a, 512).rearrange("p (i h) -> p i h", i=NT) for a in (0, 1)]
        b_prod = [area(TMP + 3072 + 512 * a, 512).rearrange("p (i h) -> p i h", i=NT) for a in (0, 1)]
        rows = area(TMP + 4096, P)
        rows2 = area(TMP + 4224, P)
        ldt2 = area(TMP + 4352, 2)
        rows_conv = area(TMP + 4360, 4 * P).rearrange("p (c n) -> p c n", c=4)
        tab = [area(TMP + 512 * a, 512).rearrange("p (e t) -> p e t", e=2) for a in (0, 1)]
        ph_a = [area(TMP + 1024 + T * a, T) for a in (0, 1)]
        ph_k = [area(TMP + 1536 + T * a, T) for a in (0, 1)]
        ph_f = [area(TMP + 2048 + T * a, T) for a in (0, 1)]
        rot_c = area(TMP + 2560, 512).rearrange("p (e t) -> p e t", e=2)
        rot_s = area(TMP + 3072, 512).rearrange("p (e t) -> p e t", e=2)
        scan_in = area(TMP + 3584, 512).rearrange("p (e t) -> p e t", e=2)
        state = [area(TMP + 4096 + 512 * a, 512).rearrange("p (e t) -> p e t", e=2) for a in (0, 1)]
        sc = [area(TMP + 768 * a, 768).rearrange("p (s c) -> p s c", s=2) for a in (0, 1)]
        att = [area(TMP + 1536 + 384 * a, 384) for a in (0, 1)]
        attT = [area(TMP + 2304 + 384 * a, 384) for a in (0, 1)]
        gate = area(TMP + 3072, 1024).rearrange("p (m t) -> p m t", t=T)
        junk_h = area(TMP + 4096, P)
        heads_out = area(0, 2048).rearrange("p (a c) -> p a c", c=P)
        xn2 = area(0, 4096).rearrange("p (t d) -> p t d", t=TT)
        xT2 = area(4096, 4096).rearrange("p (k t) -> p k t", k=KT)
        hT = area(0, FT * T).rearrange("p (k t) -> p k t", k=FT)
        ca = [area(11264 + 1024 * a, 1024).rearrange("p (m t) -> p m t", m=4) for a in (0, 1)]
        gain = area(13312, D)
        big = area(15360, D)
        xT = res[:, :].rearrange("p (k t) -> p k t", k=KT)
        x1 = res[:, :].rearrange("p (t d) -> p t d", t=TT)

        raw_in = [sem(f"raw_in{j}") for j in range(RING)]
        hi_ready = sem("hi_ready")
        lo_ready = sem("lo_ready")
        split_used = sem("split_used")
        native_used = sem("native_used")
        x_in = [sem("x_in0"), sem("x_in1")]
        rows_in, rows2_in, conv_in, rel_in = sem("rows_in"), sem("rows2_in"), sem("conv_in"), sem("rel_in")
        lam_in, b_in, c_in = sem("lam_in"), sem("b_in"), sem("c_in")
        band_out, band_in = sem("band_out"), sem("band_in")
        res_in, gain1_in, gain2_in = sem("res_in"), sem("gain1_in"), sem("gain2_in")
        out_done = sem("out_done")
        pool_ready = sem("pool_ready")
        pool_op = sem("pool_op")
        rel_mask = sem("rel_mask")
        rows_ready = sem("rows_ready")
        sq_done, std_done, rstd_done = sem("sq_done"), sem("std_done"), sem("rstd_done")
        xn_ready = sem("xn_ready")
        turn_done, turn_out = sem("turn_done"), sem("turn_out")
        xh_ready = sem("xh_ready")
        xs_ready = sem("xs_ready")
        prep_done, prep_out = sem("prep_done"), sem("prep_out")
        par_a, par_v = sem("par_a"), sem("par_v")
        lam_v, lam_a = sem("lam_v"), sem("lam_a")
        bdiag_ready = sem("bdiag_ready")
        acc_out = sem("acc_out")
        phase_ready = sem("phase_ready")
        phase_read = sem("phase_read")
        frac_ready = sem("frac_ready")
        clamp_ready = sem("clamp_ready")
        tab_abs, tab_ready = sem("tab_abs"), sem("tab_ready")
        bu_done = sem("bu_done")
        bu_used = sem("bu_used")
        tile_op = sem("tile_op")
        state_ready = sem("state_ready")
        y_done = sem("y_done")
        y_out = sem("y_out")
        gelu_done = sem("gelu_done")
        glu_hi, glu_in = sem("glu_hi"), sem("glu_in")
        sc_done, sc_read = sem("sc_done"), sem("sc_read")
        sm_op = sem("sm_op")
        neg_ready, exp_done = sem("neg_ready"), sem("exp_done")
        att_ready, att_turned, attT_ready = sem("att_ready"), sem("att_turned"), sem("attT_ready")
        av_done, av_out = sem("av_done"), sem("av_out")
        gate_ready, z_ready, z_hi, z_in = sem("gate_ready"), sem("z_ready"), sem("z_hi"), sem("z_in")
        hs_std, hs_rstd, ho_ready, ho_turned = sem("hs_std"), sem("hs_rstd"), sem("ho_ready"), sem("ho_turned")
        ho_hi, ho_in = sem("ho_hi"), sem("ho_in")
        out_scaled, out_sum = sem("out_scaled"), sem("out_sum")
        ca_ready, taps_done, silu_done, h_ready = sem("ca_ready"), sem("taps_done"), sem("silu_done"), sem("h_ready")
        hs_hi, hs_ready = sem("hs_hi"), sem("hs_ready")

        x_d = x[0].rearrange("(t p) d -> t p d", p=P)
        out_d = out[0].rearrange("(t p) d -> t p d", p=P)
        win_d = w_in[0].rearrange("(k p) n -> p k n", p=P)
        wglu_d = ssm_w_glu[0].rearrange("(k p) n -> p k n", p=P)
        wup_d = w_up[0].rearrange("(k p) n -> p k n", p=P)
        wout_d = w_out[0].rearrange("(k p) n -> k p n", p=P)
        wdown_d = w_down[0].rearrange("(k p) n -> p k n", p=P)
        in_cols = [3072, 3584] + [CH * u for u in range(6)]

        def chunk_source(c):
            if c < C_GLU:
                return win_d[:, CK * (c % 4):CK * (c % 4) + CK, in_cols[c // 4]:in_cols[c // 4] + CH]
            if c < C_OUT:
                u, half = divmod(c - C_GLU, 2)
                return wglu_d[:, CK * half:CK * half + CK, CH * u:CH * u + CH]
            return wout_d[c - C_OUT]

        def split_no(c):
            return c if c < C_QKV else c - N_QKV

        def chunk_no(s):
            return s if s < C_QKV else s + N_QKV

        def grid(ring, j):
            return ring[:, j, :].rearrange("p (k n) -> p k n", k=CK)

        def acc(unit, m):
            return ps[:, 2 * (unit % 2) + m // 2, T * (m % 2):T * (m % 2) + T]

        def acc_all(unit):
            return ps[:, 2 * (unit % 2):2 * (unit % 2) + 2, :].rearrange("p b (m t) -> p (b m) t", t=T)

        def par(name):
            return ssmp[:, PAR.index(name), :]

        PAR = ["dt", "ad", "th", "k", "r", "rc", "ab", "mag", "cos", "sin", "phi", "phi_h", "phi_l", "nr", "ni",
               "den", "t1", "t2", "fre", "fim"]
        a_re, a_im, log_dt = prm[:, 0:NT], prm[:, NT:2 * NT], prm[:, 2 * NT:3 * NT]
        gain_mix, gain_ffn = prm[:, 96:112], prm[:, 112:128]

        block = ctx.enter_context(nc.Block())

        @block.sync
        def _(sp):
            for t in range(TT):
                sp.dma_start(x_nat[:, t, :], x_d[t]).then_inc(x_in[t], 16)
            for c in range(C_UP):
                if c >= RING:
                    if C_QKV <= c - RING < C_GLU:
                        sp.wait_ge(native_used, c - RING - C_QKV + 1)
                    else:
                        sp.wait_ge(lo_ready, split_no(c - RING) + 1)
                dst = grid(raw, c % RING) if c < C_OUT else raw[:, c % RING, :]
                sp.dma_start(dst, chunk_source(c)).then_inc(raw_in[c % RING], 16)
                if c == C_GLU + 4:
                    sp.wait_ge(native_used, N_QKV)
                    for t in range(TT):
                        sp.dma_start(x1[:, t, :], x_d[t]).then_inc(res_in, 16)
                if c == C_OUT + 6:
                    sp.wait_ge(ho_in, 4)
                    sp.dma_start(gain, ln_post_mix[0:1, :].to_broadcast([P, D])).then_inc(gain1_in, 16)
            with sp.Fori(0, UNITS_FFN) as i:
                for j in range(8):
                    sp.wait_ge(lo_ready, i * 8 + (S_UP + j - RING + 1))
                    src = wup_d[:, CK * (j % 4):CK * (j % 4) + CK, bass.ds(i * CH + DFF * (j // 4), CH)]
                    sp.dma_start(grid(raw, j % RING), src).then_inc(raw_in[j % RING], 16)
            sp.wait_ge(out_sum, TT)
            sp.dma_start(gain, ln_post_ffn[0:1, :].to_broadcast([P, D])).then_inc(gain2_in, 16)
            with sp.Fori(0, FT // RING) as i:
                for j in range(RING):
                    sp.wait_ge(lo_ready, i * RING + (S_DOWN + j - RING + 1))
                    sp.dma_start(raw[:, j:j + 1, :], wdown_d[:, bass.ds(i * RING + j, 1), :])\
                        .then_inc(raw_in[j], 16)
            for t in range(TT):
                sp.wait_ge(out_sum, TT + t + 1)
                sp.dma_start(out_d[t], x1[:, t, :]).then_inc(out_done, 16)
            sp.wait_ge(out_done, 16 * TT)

        @block.gpsimd
        def _(pool):
            k = Tally(pool_ready)
            k.add(nc.gpsimd.memset(ident[:, :], 0.0))
            pool.wait_ge(pool_ready, 1)
            k.add(nc.gpsimd.affine_select(out=ident[:, :], in_=ident[:, :], compare_op=ALU.not_equal, fill=1.0,
                                          base=0, pattern=[[-1, P]], channel_multiplier=1))
            k.add(nc.gpsimd.memset(consts[:, 0:1], EPS))
            k.add(nc.gpsimd.memset(consts[:, 1:2], math.pi / 2))
            k.add(nc.gpsimd.memset(ones[:, :], 1.0))
            pool.wait_ge(pool_ready, 5)
            k.add(nc.gpsimd.memset(arena[NB:NB + 1, 8960:8960 + HEADS], NEG))
            pool.wait_ge(pool_ready, 6)
            k.add(nc.gpsimd.iota(steps[:, :], pattern=[[1, T]], base=0, channel_multiplier=0,
                                 allow_small_or_imprecise_dtypes=True))
            for a in (0, 1):
                k.add(nc.gpsimd.memset(area(4096 + 1024 * a, 1024), 0.0))
            for a in (0, 1):
                k.add(nc.gpsimd.memset(area(10240 + 1024 * a, 1024), 0.0))
            pool.wait_ge(bdiag_ready, 4)
            pool.wait_ge(prep_out, 13)

            def phases(i):
                if i >= 2:
                    pool.wait_ge(frac_ready, i - 1)
                nc.gpsimd.tensor_scalar(ph_a[i % 2], steps[:, :], par("phi_h")[:, i:i + 1], 0.0, ALU.mult, ALU.add)
                nc.gpsimd.tensor_scalar(ph_k[i % 2], steps[:, :], par("phi")[:, i:i + 1], MAGIC, ALU.mult, ALU.add)\
                    .then_inc(phase_ready, 1)

            phases(0)
            for i in range(NT):
                if i + 1 < NT:
                    phases(i + 1)
                pool.wait_ge(frac_ready, i + 1)
                nc.gpsimd.tensor_scalar(ph_f[i % 2], ph_f[i % 2], HALF_IN, -HALF_IN, ALU.min, ALU.max)\
                    .then_inc(clamp_ready, 1)

        @block.scalar
        def _(act):
            def load(dst, src, s):
                act.dma_start(dst, src).then_inc(s, 16)

            load(rows[0:32, :], ssm_a_re[0].rearrange("(i e) p -> i (e p)", e=2), rows_in)
            load(rows[32:64, :], ssm_a_im[0].rearrange("(i e) p -> i (e p)", e=2), rows_in)
            load(ldt2[64:96, :], ssm_log_dt[0].rearrange("(i e) -> i e", e=2), rows_in)
            load(rows[96:112, :], ln_pre_mix[0].rearrange("(k p) -> k p", p=P), rows_in)
            load(rows[112:128, :], ln_pre_ffn[0].rearrange("(k p) -> k p", p=P), rows_in)
            load(rows2[0:8, :], ssm_d[0].rearrange("(k g) h -> k (g h)", k=UT), rows2_in)
            load(rows2[8:9, :], attn_sub_norm[0:1, :], rows2_in)
            load(rows_conv[0:2 * FT, 0:3, :], conv_w[0].rearrange("w o (k p) -> k (w o) p", p=P), conv_in)
            load(rows_conv[0:2 * FT, 3, :], conv_b[0].rearrange("(k p) -> k p", p=P), conv_in)
            load(arena[0:NB, 8960:8960 + HEADS], rel_bias, rel_in)
            load(onehot, bucket_onehot, rel_in)
            for n, lv in enumerate((lam_q1, lam_k1, lam_q2, lam_k2)):
                load(lamt[0:1, n, :], lv[0:1, :], lam_in)
            for a, cw in enumerate((ssm_c_re, ssm_c_im)):
                for e in (0, 1):
                    load(c_nat[a][:, :, e, :], cw[0].rearrange("g h p -> (g h) p").rearrange("(j r) p -> r j p", r=P),
                         c_in)
            for a, bw in enumerate((ssm_b_re, ssm_b_im)):
                load(b_nat[a], bw[0].rearrange("g p h -> (g p) h").rearrange("(i q) h -> q i h", q=P), b_in)

            def squares(n, src, scratch):
                for t in range(TT):
                    act.wait_ge(sq_done, TT * n + t)
                    nc.scalar.activation(scratch, src(t), ACT.Square, accum_out=stat[:, n, 0, t:t + 1])\
                        .then_inc(sq_done, 1)
                act.wait_ge(sq_done, TT * (n + 1))
                nc.scalar.activation(stat[:, n, 1, :], stat[:, n, 0, :], ACT.Sqrt, bias=consts[:, 0:1],
                                     scale=1.0 / D).then_inc(std_done, 1)

            def take_turned(n, dst, gains):
                for g in range(8):
                    act.wait_ge(turn_done, 8 * n + g + 1)
                    for kk in range(2):
                        last = nc.scalar.activation(dst[:, 2 * g + kk, :], ps[:, g % 4, T * kk:T * kk + T],
                                                    ACT.Identity, scale=gains[:, 2 * g + kk:2 * g + kk + 1])
                    last.then_inc(turn_out, 1)

            def hi(s):
                c = chunk_no(s)
                act.wait_ge(raw_in[c % RING], 16 * (c // RING + 1))
                if s >= RING:
                    act.wait_ge(split_used, s - RING + 1)
                nc.scalar.copy(w_hi[:, c % RING, :], raw[:, c % RING, :]).then_inc(hi_ready, 1)

            def prep(n):
                act.wait_ge(prep_done, n + 1)
                return ps[:, 4 + n % 4, :]

            act.wait_ge(pool_ready, 11)
            act.wait_ge(x_in[0], 16)
            act.wait_ge(x_in[1], 16)
            squares(0, lambda t: x_nat[:, t, :], junk)
            nc.scalar.copy(prm[:, :], prep(0)[:, 0:P]).then_inc(prep_out, 1)
            act.wait_ge(prep_out, 1)
            take_turned(0, xT, gain_mix)
            for s in range(RING):
                hi(s)
            nc.scalar.copy(prm2[:, :], prep(1)[:, 0:UT + 1]).then_inc(prep_out, 1)
            nc.scalar.copy(conv[:, :, :], prep(2)[:, 0:8 * FT].rearrange("p (c k) -> p c k", c=4)).then_inc(prep_out, 1)
            nc.scalar.copy(bandrow, prep(3)[0:HEADS, 0:BAND]).then_inc(prep_out, 1)
            act.wait_ge(prep_out, 4)
            act.dma_start(band_dram, bandrow.unsqueeze(1).to_broadcast([HEADS, P, BAND])).then_inc(band_out, 16)
            for a in (0, 1):
                for q in (0, 1):
                    src = prep(4 + 2 * a + q).rearrange("p (i e h) -> p i e h", e=2, h=HC)
                    for e in (0, 1):
                        half = slice(PS * e, PS * e + PS)
                        last = nc.scalar.activation(CS[a][half, 16 * q:16 * q + 16, e, :], src[half, :, e, :],
                                                    ACT.Identity, scale=1.0 - 2.0 * a)
                    last.then_inc(prep_out, 1)
            nc.scalar.activation(par("dt"), log_dt, ACT.Exp).then_inc(par_a, 1)
            act.wait_ge(lam_v, 2)
            nc.scalar.activation(lams[:, 2:4], lams[:, 0:2], ACT.Exp).then_inc(lam_a, 1)
            act.wait_ge(par_v, 1)
            nc.scalar.activation(par("mag"), par("ad"), ACT.Exp).then_inc(par_a, 1)
            act.wait_ge(par_v, 9)
            nc.scalar.activation(par("sin"), par("rc"), ACT.Sin).then_inc(par_a, 1)
            nc.scalar.activation(par("cos"), par("ab"), ACT.Sin, bias=consts[:, 1:2], scale=-1.0).then_inc(par_a, 1)
            for s in range(RING, 2 * RING):
                hi(s)
            nc.scalar.copy(lam_col[:, :], prep(8)[:, 0:1]).then_inc(prep_out, 1)
            act.wait_ge(band_out, 16)
            for a in (0, 1):
                for q in (0, 1):
                    nc.scalar.copy(BT[a][:, 4 * q:4 * q + 4, :],
                                   prep(9 + 2 * a + q).rearrange("p (j q) -> p j q", j=4)).then_inc(prep_out, 1)
            for u in range(2):
                act.wait_ge(split_used, 4 * (u + 1))
                nc.scalar.copy(uT[:, 4 * u:4 * u + 4, :], acc_all(u)).then_inc(acc_out, 1)

            def table(i):
                act.wait_ge(clamp_ready, i + 1)
                if i >= 2:
                    act.wait_ge(state_ready, i - 1)
                nc.scalar.activation(tab[i % 2][:, 0, :], ph_f[i % 2], ACT.Abs).then_inc(tab_abs, 1)
                nc.scalar.activation(tab[i % 2][:, 1, :], ph_f[i % 2], ACT.Sin, scale=2 * math.pi)
                act.wait_ge(tab_abs, i + 1)
                nc.scalar.activation(tab[i % 2][:, 0, :], tab[i % 2][:, 0, :], ACT.Sin, bias=consts[:, 1:2],
                                     scale=-2 * math.pi).then_inc(tab_ready, 1)

            def take_qkv(u):
                act.wait_ge(native_used, 4 * (u + 1))
                if u < 4:
                    dst = (qT if u < 2 else kT)[:, 4 * (u % 2):4 * (u % 2) + 4, :]
                    nc.scalar.copy(dst, acc_all(u)).then_inc(acc_out, 1)
                else:
                    nc.scalar.copy(v[:, :, CH * (u - 4):CH * (u - 4) + CH], ps[:, 2 * (u % 2):2 * (u % 2) + 2, :])\
                        .then_inc(acc_out, 1)

            units = 0
            for i in range(NT):
                table(i)
                if i == 16 * (units + 1) // 3:
                    take_qkv(units)
                    units += 1
            for u in range(units, 6):
                take_qkv(u)
            for s in range(S_GLU, S_GLU + RING):
                hi(s)
            act.wait_ge(y_out, UT)
            act.wait_ge(band_out, 16)
            shifted = lambda m, n: bass.AP(band_dram.tensor, P - 1 + m, [[BAND - 1, P], [P * BAND, HEADS], [1, n]])
            act.dma_start(band[:, :, 0:P], shifted(P, P)).then_inc(band_in, 16)
            act.dma_start(band[:, :, P:P + T], shifted(0, T)).then_inc(band_in, 16)
            nc.scalar.activation(uT, uT, ACT.Gelu_apprx_tanh).then_inc(gelu_done, 1)
            act.wait_ge(gelu_done, 1)
            nc.scalar.copy(xs[:, UT:KT, 0, :], uT).then_inc(glu_hi, 1)

            def take_attT(h):
                act.wait_ge(att_turned, h + 1)
                if h >= 2:
                    act.wait_ge(av_done, h - 1)
                nc.scalar.copy(attT[h % 2], ps[:, 6, 0:384]).then_inc(attT_ready, 1)

            def take_head(h):
                act.wait_ge(av_done, h + 1)
                nc.scalar.copy(heads_out[:, TT * h:TT * h + TT, :],
                               ps[:, 7, 0:T].rearrange("p (t c) -> p t c", t=TT))
                for t in range(TT):
                    act.wait_ge(hs_std, TT * h + t)
                    nc.scalar.activation(junk_h, ps[:, 7, P * t:P * t + P], ACT.Square,
                                         accum_out=heads_stat[:, 0, TT * h + t:TT * h + t + 1]).then_inc(hs_std, 1)

            for c in range(HEADS + 1):
                if c < HEADS:
                    act.wait_ge(neg_ready, c + 1)
                    for s in (0, 1):
                        for t, cols in ((0, slice(0, P)), (1, slice(P, P + T))):
                            last = nc.scalar.activation(sc[c % 2][:, s, cols], sc[c % 2][:, s, cols], ACT.Exp,
                                                        bias=sm[:, c % 2, 1, t, s:s + 1],
                                                        accum_out=sm[:, c % 2, 2, t, s:s + 1])
                    last.then_inc(exp_done, 1)
                if c >= 1:
                    take_attT(c - 1)
                if c < HEADS:
                    hi(S_GLU + RING + c)
                if c >= 1:
                    take_head(c - 1)
                if c < HEADS and c % 2:
                    u = c // 2
                    act.wait_ge(split_used, S_GLU + c + 1)
                    if u < 2:
                        nc.scalar.copy(zT[:, 4 * u:4 * u + 4, :], acc_all(u)).then_inc(acc_out, 1)
                    else:
                        if u == 3:
                            act.wait_ge(z_ready, 1)
                        nc.scalar.activation(gate, acc_all(u), ACT.Sigmoid).then_inc(acc_out, 1)
            act.wait_ge(hs_std, HEADS * TT)
            nc.scalar.activation(heads_stat[:, 1, :], heads_stat[:, 0, :], ACT.Sqrt, bias=consts[:, 0:1],
                                 scale=1.0 / P).then_inc(hs_std, 1)
            act.wait_ge(z_ready, 2)
            nc.scalar.copy(xs[:, UT:KT, 0, :], zT).then_inc(z_hi, 1)
            for b in range(4):
                act.wait_ge(ho_turned, b + 1)
                nc.scalar.activation(xs[:, 2 * b:2 * b + 2, 0, :], ps[:, 4 + b, :].rearrange("p (m t) -> p m t", t=T),
                                     ACT.Identity, scale=gain_o[:, 0:1]).then_inc(ho_hi, 1)
            for s in range(S_OUT + RING, S_UP):
                hi(s)
            for s in range(S_UP, S_UP + RING):
                hi(s)
            squares(1, lambda t: ps[:, 4 * t:4 * t + 4, :].rearrange("p b n -> p (b n)"), big)
            act.wait_ge(out_sum, TT)
            squares(2, lambda t: x1[:, t, :], big)
            take_turned(1, xT2, gain_ffn)

            def hi_loop(j, s, loads):
                act.wait_ge(raw_in[j], loads)
                act.wait_ge(split_used, s)
                nc.scalar.copy(w_hi[:, j, :], raw[:, j, :]).then_inc(hi_ready, 1)

            def first_tap(i, a):
                act.wait_ge(split_used, i * 8 + (S_UP + 4 * a + 4))
                if a == 0:
                    act.wait_ge(h_ready, i + 1)
                for m in range(4):
                    col = i * 4 + (m + FT * a)
                    last = nc.scalar.activation(ca[a][:, m, :], acc(a, m), ACT.Identity,
                                                scale=conv[:, 2, bass.ds(col, 1)], bias=conv[:, 3, bass.ds(col, 1)])
                    if m % 2:
                        last.then_inc(ca_ready, 1)

            with act.Fori(0, UNITS_FFN) as i:
                for j in range(RING):
                    hi_loop(j, i * 8 + (S_UP + j + 1), i * 32 + 16 * (C_UP // RING + 2))
                first_tap(i, 0)
                for j in range(RING):
                    hi_loop(j, i * 8 + (S_UP + RING + j + 1), i * 32 + 16 * (C_UP // RING + 3))
                first_tap(i, 1)
                act.wait_ge(taps_done, i * 16 + 9)
                nc.scalar.activation(ca[0], ca[0], ACT.Silu).then_inc(silu_done, 1)

            def hidden_hi(j, k):
                nc.scalar.copy(xs[:, j:j + 1, 0, :], hT[:, k, :]).then_inc(hs_hi, 1)

            act.wait_ge(h_ready, UNITS_FFN + 1)
            for j in range(RING):
                hidden_hi(j, slice(j, j + 1))
            with act.Fori(0, FT // RING - 1) as i:
                for j in range(RING):
                    hi_loop(j, i * RING + (S_DOWN + j + 1), i * 16 + 16 * (C_UP // RING + 22 + 2))
                    hidden_hi(j, bass.ds(i * RING + (RING + j), 1))
            act.wait_ge(split_used, S_DOWN + FT)
            squares(3, lambda t: ps[:, 4 * t:4 * t + 4, :].rearrange("p b n -> p (b n)"), area(0, D))

        @block.vector
        def _(dve):
            V = nc.vector

            def rstd(n):
                dve.wait_ge(std_done, n + 1)
                V.reciprocal(stat[:, n, 2, :], stat[:, n, 1, :]).then_inc(rstd_done, 1)
                dve.wait_ge(rstd_done, n + 1)

            def scale_rows(n, dst, src):
                for t in range(TT):
                    V.tensor_scalar(dst[:, t, :], src[:, t, :], stat[:, n, 2, t:t + 1], None, ALU.mult)\
                        .then_inc(xn_ready, 1)

            def split_turned(n, src):
                for g in range(9):
                    if g < 8:
                        dve.wait_ge(turn_out, 8 * n + g + 1)
                        V.tensor_copy(xs[:, 2 * g:2 * g + 2, 0, :], src[:, 2 * g:2 * g + 2, :]).then_inc(xh_ready, 1)
                    if g >= 1:
                        dve.wait_ge(xh_ready, 8 * n + g)
                        V.tensor_tensor(xs[:, 2 * g - 2:2 * g, 1, :], src[:, 2 * g - 2:2 * g, :],
                                        xs[:, 2 * g - 2:2 * g, 0, :].bitcast(F32), ALU.subtract)\
                            .then_inc(xs_ready, 1)

            def lo(s):
                j = chunk_no(s) % RING
                dve.wait_ge(hi_ready, s + 1)
                V.tensor_tensor(w_lo[:, j, :], raw[:, j, :], w_hi[:, j, :].bitcast(F32), ALU.subtract)\
                    .then_inc(lo_ready, 1)

            dve.wait_ge(rows_in, 16 * 5)
            V.tensor_copy(rows[64:96, :].rearrange("p (e q) -> p e q", e=2),
                          ldt2[64:96, :].unsqueeze(2).to_broadcast([32, 2, PS])).then_inc(rows_ready, 1)
            rstd(0)
            scale_rows(0, x_nat, x_nat)
            split_turned(0, xT)
            for s in range(RING):
                lo(s)

            lv = Tally(lam_v)
            dve.wait_ge(lam_in, 16 * 4)
            for n in (0, 1):
                if n:
                    dve.wait_ge(lam_v, 1)
                lv.add(V.tensor_tensor_reduce(out=lamj[:, :], in0=lamt[0:1, 2 * n, :], in1=lamt[0:1, 2 * n + 1, :],
                                              scale=1.0, scalar=0.0, op0=ALU.mult, op1=ALU.add,
                                              accum_out=lams[0:1, n:n + 1]))
            pv = Tally(par_v)

            def step(ins):
                dve.wait_ge(par_v, pv.add(ins))

            dve.wait_ge(prep_out, 2)
            V.tensor_scalar(gain_o[:, :], prm2[:, UT:UT + 1], 1.0 - LAMBDA_INIT, None, ALU.mult)
            dve.wait_ge(par_a, 1)
            step(V.tensor_tensor(par("ad"), a_re, par("dt"), ALU.mult))
            step(V.tensor_tensor(par("th"), a_im, par("dt"), ALU.mult))
            step(V.tensor_scalar(par("k"), par("th"), INV2PI, MAGIC, ALU.mult, ALU.add))
            step(V.tensor_scalar(par("k"), par("k"), MAGIC, None, ALU.subtract))
            for n, part in enumerate((PI_A, PI_B, PI_C)):
                step(V.scalar_tensor_tensor(par("r"), par("k"), -part, par("th" if n == 0 else "r"),
                                            ALU.mult, ALU.add))
            step(V.tensor_scalar(par("rc"), par("r"), PI_IN, -PI_IN, ALU.min, ALU.max))
            step(V.scalar_tensor_tensor(par("ab"), par("rc"), -1.0, par("rc"), ALU.mult, ALU.max))
            step(V.tensor_scalar(par("phi"), par("r"), INV2PI, None, ALU.mult))
            step(V.tensor_scalar(par("phi_h"), par("phi"), MAGIC16, MAGIC16, ALU.add, ALU.subtract))
            for n, part in enumerate((PI_A, PI_B, PI_C)):
                step(V.scalar_tensor_tensor(par("phi_l"), par("phi_h"), -part, par("r" if n == 0 else "phi_l"),
                                            ALU.mult, ALU.add))
            step(V.tensor_scalar(par("phi_l"), par("phi_l"), INV2PI, None, ALU.mult))
            step(V.tensor_tensor(par("den"), a_re, a_re, ALU.mult))
            step(V.tensor_tensor(par("t1"), a_im, a_im, ALU.mult))
            step(V.tensor_tensor(par("den"), par("den"), par("t1"), ALU.add))
            step(V.reciprocal(par("den"), par("den")))
            dve.wait_ge(par_a, 4)
            step(V.tensor_tensor(par("nr"), par("mag"), par("cos"), ALU.mult))
            step(V.tensor_scalar(par("nr"), par("nr"), 1.0, None, ALU.subtract))
            step(V.tensor_tensor(par("ni"), par("mag"), par("sin"), ALU.mult))
            step(V.tensor_tensor(par("t1"), par("nr"), a_re, ALU.mult))
            step(V.tensor_tensor(par("t2"), par("ni"), a_im, ALU.mult))
            step(V.tensor_tensor(par("t1"), par("t1"), par("t2"), ALU.add))
            step(V.tensor_tensor(par("fre"), par("t1"), par("den"), ALU.mult))
            step(V.tensor_tensor(par("t1"), par("ni"), a_re, ALU.mult))
            step(V.tensor_tensor(par("t2"), par("nr"), a_im, ALU.mult))
            step(V.tensor_tensor(par("t1"), par("t1"), par("t2"), ALU.subtract))
            step(V.tensor_tensor(par("fim"), par("t1"), par("den"), ALU.mult))
            dve.wait_ge(b_in, 32)
            dve.wait_ge(pool_ready, 11)
            for a, (f0, f1, op) in enumerate((("fre", "fim", ALU.subtract), ("fim", "fre", ALU.add))):
                for n, f in enumerate((f0, f1)):
                    step(V.tensor_tensor(b_prod[n], b_nat[n], par(f).unsqueeze(2).to_broadcast([P, NT, HC]), ALU.mult))
                for e in (0, 1):
                    half = slice(PS * e, PS * e + PS)
                    V.tensor_tensor(b_diag[a][half, :, e, :], b_prod[0][half], b_prod[1][half], op)\
                        .then_inc(bdiag_ready, 1)
                dve.wait_ge(bdiag_ready, 2 * a + 2)
            dve.wait_ge(lam_a, 1)
            lv.add(V.tensor_tensor(lams[:, 4:5], lams[:, 2:3], lams[:, 3:4], ALU.subtract))
            dve.wait_ge(lam_v, 3)
            lv.add(V.tensor_scalar(lams[:, 5:6], lams[:, 4:5], LAMBDA_INIT, -1.0, ALU.add, ALU.mult))
            for s in range(RING, 2 * RING):
                lo(s)

            def phase(i):
                f = ph_f[i % 2]
                dve.wait_ge(phase_ready, i + 1)
                if i >= 2:
                    dve.wait_ge(tab_ready, i - 1)
                V.scalar_tensor_tensor(f, ph_k[i % 2], MAGIC, ph_a[i % 2], ALU.subtract, ALU.subtract)\
                    .then_inc(phase_read, 1)
                dve.wait_ge(phase_read, i + 1)
                V.scalar_tensor_tensor(f, steps[:, :], par("phi_l")[:, i:i + 1], f, ALU.mult, ALU.subtract)\
                    .then_inc(frac_ready, 1)

            def add_skip(j):
                dve.wait_ge(y_done, 4 * j + 4)
                V.scalar_tensor_tensor(uT[:, j, :], uT[:, j, :], prm2[:, j:j + 1], ps[:, 6 + j % 2, 0:T],
                                       ALU.mult, ALU.add).then_inc(y_out, 1)

            top = Tally(tile_op)
            phase(0)
            phase(1)
            for i in range(NT):
                bu = ps[:, 4 + i % 2, :].rearrange("p (e t) -> p e t", e=2)
                cos2 = tab[i % 2][:, 0:1, :].to_broadcast([P, 2, T])
                sin2 = tab[i % 2][:, 1:2, :].to_broadcast([P, 2, T])
                decay = par("mag")[:, i:i + 1].to_broadcast([P, T])
                dve.wait_ge(tab_ready, i + 1)
                dve.wait_ge(bu_done, i + 1)
                top.add(V.tensor_tensor(rot_c, bu, cos2, ALU.mult))
                V.tensor_tensor(rot_s, bu, sin2, ALU.mult).then_inc(bu_used, 1)
                dve.wait_ge(tile_op, top.n)
                dve.wait_ge(bu_used, i + 1)
                re_in = top.add(V.tensor_tensor(scan_in[:, 0, :], rot_c[:, 0, :], rot_s[:, 1, :], ALU.add))
                im_in = top.add(V.tensor_tensor(scan_in[:, 1, :], rot_c[:, 1, :], rot_s[:, 0, :], ALU.subtract))
                dve.wait_ge(tile_op, re_in)
                dve.wait_ge(tile_op, im_in)
                top.add(V.tensor_tensor_scan(rot_c[:, 0, :], decay, scan_in[:, 0, :], 0.0, ALU.mult, ALU.add))
                top.add(V.tensor_tensor_scan(rot_c[:, 1, :], decay, scan_in[:, 1, :], 0.0, ALU.mult, ALU.add))
                dve.wait_ge(tile_op, top.n)
                top.add(V.tensor_tensor(scan_in, rot_c, cos2, ALU.mult))
                top.add(V.tensor_tensor(rot_s, rot_c, sin2, ALU.mult))
                dve.wait_ge(tile_op, top.n)
                if i >= 2:
                    dve.wait_ge(y_done, i - 1)
                top.add(V.tensor_tensor(state[i % 2][:, 0, :], scan_in[:, 0, :], rot_s[:, 1, :], ALU.subtract))
                V.tensor_tensor(state[i % 2][:, 1, :], scan_in[:, 1, :], rot_s[:, 0, :], ALU.add)\
                    .then_inc(state_ready, 1)
                dve.wait_ge(state_ready, i + 1)
                if i + 2 < NT:
                    phase(i + 2)
                if i % 4 == 1 and i > 4:
                    add_skip(i // 4 - 1)
            add_skip(UT - 1)
            for s in range(S_GLU, S_GLU + RING):
                lo(s)
            dve.wait_ge(glu_hi, 1)
            V.tensor_tensor(xs[:, UT:KT, 1, :], uT, xs[:, UT:KT, 0, :].bitcast(F32), ALU.subtract).then_inc(glu_in, 1)

            so = Tally(sm_op)
            TILES = ((0, slice(0, P)), (1, slice(P, P + T)))
            dve.wait_ge(band_in, 32)
            dve.wait_ge(prep_out, 9)
            for h in range(HEADS):
                e, st = sc[h % 2], sm[:, h % 2]
                dve.wait_ge(sc_done, h + 1)
                for s in (0, 1):
                    V.scalar_tensor_tensor(e[:, s, :], ps[:, 4 + s, 0:384], DH ** -0.5, band[:, h, :],
                                           ALU.mult, ALU.add).then_inc(sc_read, 1)
                dve.wait_ge(sc_read, 2 * h + 2)
                for t, cols in TILES:
                    so.add(V.tensor_reduce(st[:, 0, t, :], e[:, :, cols], AX.X, ALU.max))
                dve.wait_ge(sm_op, so.n)
                V.tensor_scalar(st[:, 1, :, :], st[:, 0, :, :], -1.0, None, ALU.mult).then_inc(neg_ready, 1)
                lo(S_GLU + RING + h)
                dve.wait_ge(exp_done, h + 1)
                so.add(V.reciprocal(st[:, 3, :, :], st[:, 2, :, :]))
                dve.wait_ge(sm_op, so.n)
                so.add(V.tensor_scalar(st[:, 4, :, :], st[:, 3, :, :], lam_col[:, 0:1], None, ALU.mult))
                dve.wait_ge(sm_op, so.n)
                for t, cols in TILES:
                    so.add(V.tensor_scalar(e[:, 1, cols], e[:, 1, cols], st[:, 4, t, 1:2], None, ALU.mult))
                dve.wait_ge(sm_op, so.n)
                if h >= 2:
                    dve.wait_ge(att_turned, h - 1)
                for t, cols in TILES:
                    V.scalar_tensor_tensor(att[h % 2][:, cols], e[:, 0, cols], st[:, 3, t, 0:1], e[:, 1, cols],
                                           ALU.mult, ALU.add).then_inc(att_ready, 1)
                if h >= 6:
                    u = h - 6
                    dve.wait_ge(acc_out, 8 + 2 + u + 1)
                    V.tensor_tensor(zT[:, 4 * u:4 * u + 4, :], zT[:, 4 * u:4 * u + 4, :], gate, ALU.mult)\
                        .then_inc(z_ready, 1)
            dve.wait_ge(hs_std, HEADS * TT + 1)
            V.reciprocal(heads_stat[:, 2, :], heads_stat[:, 1, :]).then_inc(hs_rstd, 1)
            dve.wait_ge(hs_rstd, 1)
            V.tensor_tensor(heads_out, heads_out, heads_stat[:, 2, :].unsqueeze(2).to_broadcast([P, HEADS * TT, P]),
                            ALU.mult).then_inc(ho_ready, 1)
            dve.wait_ge(z_hi, 1)
            V.tensor_tensor(xs[:, UT:KT, 1, :], zT, xs[:, UT:KT, 0, :].bitcast(F32), ALU.subtract).then_inc(z_in, 1)
            for b in range(4):
                dve.wait_ge(ho_hi, b + 1)
                V.scalar_tensor_tensor(xs[:, 2 * b:2 * b + 2, 1, :], ps[:, 4 + b, :].rearrange("p (m t) -> p m t", t=T),
                                       gain_o[:, 0:1], xs[:, 2 * b:2 * b + 2, 0, :].bitcast(F32),
                                       ALU.mult, ALU.subtract).then_inc(ho_in, 1)
            for s in range(S_OUT + RING, S_UP + RING):
                lo(s)

            def post_norm(n, tmp, gain_here, base):
                rstd(n)
                gain_here()
                for t in range(TT):
                    V.scalar_tensor_tensor(tmp[:, t, :], ps[:, 4 * t:4 * t + 4, :].rearrange("p b n -> p (b n)"),
                                           stat[:, n, 2, t:t + 1], gain, ALU.mult, ALU.mult).then_inc(out_scaled, 1)
                for t in range(TT):
                    dve.wait_ge(out_scaled, base + t + 1)
                    V.tensor_tensor(x1[:, t, :], x1[:, t, :], tmp[:, t, :], ALU.add).then_inc(out_sum, 1)

            dve.wait_ge(res_in, 32)
            post_norm(1, xn2, lambda: dve.wait_ge(gain1_in, 16), 0)
            dve.wait_ge(out_sum, TT)
            rstd(2)
            scale_rows(2, xn2, x1)
            split_turned(1, xT2)

            def lo_loop(j, s):
                dve.wait_ge(hi_ready, s)
                V.tensor_tensor(w_lo[:, j, :], raw[:, j, :], w_hi[:, j, :].bitcast(F32), ALU.subtract)\
                    .then_inc(lo_ready, 1)

            def older_taps(i, a):
                for b in (0, 1):
                    dve.wait_ge(ca_ready, i * 4 + (2 * a + b + 1))
                    for tap in (1, 0):
                        back = 2 - tap
                        if tap == 0:
                            dve.wait_ge(taps_done, i * 16 + (8 * a + 4 * b + 3))
                        for m in (2 * b, 2 * b + 1):
                            col = i * 4 + (m + FT * a)
                            V.scalar_tensor_tensor(ca[a][:, m, back:T], acc(a, m)[:, 0:T - back],
                                                   conv[:, tap, bass.ds(col, 1)], ca[a][:, m, back:T],
                                                   ALU.mult, ALU.add).then_inc(taps_done, 1)

            dve.sem_inc(taps_done, 1)
            dve.sem_inc(h_ready, 1)
            with dve.Fori(0, UNITS_FFN) as i:
                for j in range(RING):
                    lo_loop(j, i * 8 + (S_UP + RING + j + 1))
                older_taps(i, 0)
                for j in range(RING):
                    lo_loop(j, i * 8 + (S_UP + 2 * RING + j + 1))
                older_taps(i, 1)
                dve.wait_ge(taps_done, i * 16 + 17)
                dve.wait_ge(silu_done, i + 1)
                V.tensor_tensor(hT[:, bass.ds(i * 4, 4), :], ca[0], ca[1], ALU.mult).then_inc(h_ready, 1)

            def hidden_lo(j, k, n):
                dve.wait_ge(hs_hi, n)
                V.tensor_tensor(xs[:, j:j + 1, 1, :], hT[:, k, :], xs[:, j:j + 1, 0, :].bitcast(F32), ALU.subtract)\
                    .then_inc(hs_ready, 1)

            for j in range(RING):
                hidden_lo(j, slice(j, j + 1), j + 1)
            with dve.Fori(0, FT // RING - 1) as i:
                for j in range(RING):
                    lo_loop(j, i * RING + (S_DOWN + RING + j + 1))
                    hidden_lo(j, bass.ds(i * RING + (RING + j), 1), i * RING + (RING + j + 1))
            post_norm(3, xn2, lambda: dve.wait_ge(gain2_in, 16), TT)

        @block.tensor
        def _(pe):
            mm = nc.tensor.matmul

            def turn(n, src):
                pe.wait_ge(xn_ready, TT * (n + 1))
                for g in range(8):
                    if g >= 4:
                        pe.wait_ge(turn_out, 8 * n + g - 3)
                    for kk in range(2):
                        for t in range(TT):
                            k = 2 * g + kk
                            last = nc.tensor.transpose(ps[:, g % 4, T * kk + P * t:T * kk + P * t + P],
                                                       src[:, t, P * k:P * k + P], ident[:, :])
                    last.then_inc(turn_done, 1)

            def channels_chunk(j, unit, k0, first, last_chunk, act_k0):
                hi_w, lo_w = grid(w_hi, j), grid(w_lo, j)
                for kk in range(CK):
                    start, stop = first and kk == 0, last_chunk and kk == CK - 1
                    x_hi, x_lo = xs[:, act_k0 + k0 + kk, 0, :], xs[:, act_k0 + k0 + kk, 1, :]
                    for m in range(4):
                        w = slice(P * m, P * m + P)
                        mm(acc(unit, m), hi_w[:, kk, w], x_hi, start=start and m % 2 == 0, stop=False,
                           skip_group_check=True)
                        mm(acc(unit, m), hi_w[:, kk, w], x_lo, start=False, stop=False, skip_group_check=True)
                        last = mm(acc(unit, m), lo_w[:, kk, w], x_hi, start=False, stop=stop, skip_group_check=True)
                last.then_inc(split_used, 1)

            def tokens_chunk(j, k, start, stop):
                for t in range(TT):
                    x_hi, x_lo = xs[:, k, 0, P * t:P * t + P], xs[:, k, 1, P * t:P * t + P]
                    for stat_op, ring, first, end in ((x_hi, w_hi, True, False), (x_hi, w_lo, False, False),
                                                      (x_lo, w_hi, False, True)):
                        for n in range(4):
                            last = mm(ps[:, 4 * t + n, :], stat_op, ring[:, j, CH * n:CH * n + CH],
                                      start=start and first, stop=stop and end)
                last.then_inc(split_used, 1)

            pe.wait_ge(pool_ready, 11)
            pe.wait_ge(rows_in, 16 * 5)
            pe.wait_ge(rows_ready, 1)
            nc.tensor.transpose(ps[:, 4, 0:P], rows, ident[:, :]).then_inc(prep_done, 1)
            turn(0, x_nat)

            def u_chunk(c):
                pe.wait_ge(xs_ready, min(8, 2 * (c % 4) + 2))
                pe.wait_ge(lo_ready, c + 1)
                channels_chunk(c % RING, c // 4, CK * (c % 4), c % 4 == 0, c % 4 == 3, 0)

            pe.wait_ge(turn_out, 8)
            u_chunk(0)
            pe.wait_ge(rows2_in, 32)
            nc.tensor.transpose(ps[:, 5, 0:UT + 1], rows2[0:UT + 1, :], ident[0:UT + 1, 0:UT + 1])\
                .then_inc(prep_done, 1)
            pe.wait_ge(conv_in, 32)
            for n in range(4):
                last = nc.tensor.transpose(ps[:, 6, 2 * FT * n:2 * FT * n + 2 * FT], rows_conv[0:2 * FT, n, :],
                                           ident[0:2 * FT, 0:2 * FT])
            last.then_inc(prep_done, 1)
            pe.wait_ge(rel_in, 32)
            mm(ps[0:HEADS, 7, 0:BAND], relb, onehot, start=True, stop=True).then_inc(prep_done, 1)
            pe.wait_ge(c_in, 64)
            for n in range(4, 8):
                a, q = divmod(n - 4, 2)
                pe.wait_ge(prep_out, n - 3)
                for j in range(4):
                    last = nc.tensor.transpose(ps[:, 4 + n % 4, P * j:P * j + P],
                                               c_nat[a][:, 4 * q + j, :, :].rearrange("p e q -> p (e q)"), ident[:, :])
                last.then_inc(prep_done, 1)
            for c in range(1, 4):
                u_chunk(c)
            pe.wait_ge(lam_v, 4)
            pe.wait_ge(prep_out, 5)
            mm(ps[:, 4, 0:1], ones[:, :], lams[:, 5:6], start=True, stop=True).then_inc(prep_done, 1)
            pe.wait_ge(bdiag_ready, 4)
            for n in range(9, 13):
                a, q = divmod(n - 9, 2)
                pe.wait_ge(prep_out, n - 3)
                for j in range(4):
                    jj = 4 * q + j
                    last = nc.tensor.transpose(ps[:, 4 + n % 4, P * j:P * j + P],
                                               b_diag[a][:, 4 * jj:4 * jj + 4, :, :].rearrange("p i e h -> p (i e h)"),
                                               ident[:, :])
                last.then_inc(prep_done, 1)
            for c in range(4, 8):
                u_chunk(c)

            def b_u(i):
                q, j = 32 * (i % 4), i // 4
                if i >= 2:
                    pe.wait_ge(bu_used, i - 1)
                for a in (0, 1):
                    last = mm(ps[:, 4 + i % 2, T * a:T * a + T], BT[a][q:q + 32, j, :], uT[q:q + 32, j, :],
                              start=True, stop=True)
                last.then_inc(bu_done, 1)

            def c_x(i):
                q, j = 32 * (i % 4), i // 4
                pe.wait_ge(state_ready, i + 1)
                if j >= 2:
                    pe.wait_ge(y_out, j - 1)
                for a in (0, 1):
                    last = mm(ps[q:q + 32, 6 + j % 2, 0:T], CS[a][:, i, :, :].rearrange("p e h -> p (e h)"),
                              state[i % 2][:, a, :], start=a == 0, stop=a == 1)
                last.then_inc(y_done, 1)

            pe.wait_ge(acc_out, 2)
            pe.wait_ge(prep_out, 13)
            for s in range(4 * N_QKV):
                unit, k = divmod(s, KT)
                c, kk = divmod(s, CK)
                slot = (C_QKV + c) % RING
                if kk == 0:
                    pe.wait_ge(raw_in[slot], 16 * ((C_QKV + c) // RING + 1))
                if k == 0:
                    pe.wait_ge(acc_out, 2 + max(0, unit - 1))
                w = grid(raw, slot)[:, kk, :]
                for m in range(4):
                    if unit < 4:
                        last = mm(acc(unit, m), w[:, P * m:P * m + P], xT[:, k, :], start=k == 0 and m % 2 == 0,
                                  stop=k == KT - 1, skip_group_check=True)
                    elif m < TT:
                        last = mm(ps[:, 2 * (unit % 2) + m, :], xT[:, k, P * m:P * m + P], w, start=k == 0,
                                  stop=k == KT - 1)
                if kk == CK - 1:
                    last.then_inc(native_used, 1)
                if s % 3 == 0:
                    b_u(s // 3)
                    if s // 3 >= 2:
                        c_x(s // 3 - 2)
            c_x(NT - 2)
            c_x(NT - 1)

            def scores(h):
                if h == 0:
                    pe.wait_ge(acc_out, 8)
                else:
                    pe.wait_ge(sc_read, 2 * h)
                for s in (0, 1):
                    half = slice(DH * s, DH * s + DH)
                    mm(ps[:, 4 + s, 0:P], qT[half, h, 0:P], kT[half, h, 0:P], start=True, stop=True)
                    last = mm(ps[:, 4 + s, P:P + T], qT[half, h, P:T], kT[half, h, :], start=True, stop=True)
                last.then_inc(sc_done, 1)

            def turn_att(h):
                pe.wait_ge(att_ready, 2 * h + 2)
                if h >= 1:
                    pe.wait_ge(attT_ready, h)
                for b in range(3):
                    last = nc.tensor.transpose(ps[:, 6, P * b:P * b + P], att[h % 2][:, P * b:P * b + P], ident[:, :])
                last.then_inc(att_turned, 1)

            def att_v(h):
                pe.wait_ge(attT_ready, h + 1)
                if h >= 1:
                    pe.wait_ge(hs_std, TT * h)
                cols = slice(P * h, P * h + P)
                mm(ps[:, 7, 0:P], attT[h % 2][:, 0:P], v[:, 0, cols], start=True, stop=True)
                mm(ps[:, 7, P:T], attT[h % 2][:, P:T], v[:, 0, cols], start=True, stop=False)
                mm(ps[:, 7, P:T], attT[h % 2][:, T:T + P], v[:, 1, cols], start=False, stop=True)\
                    .then_inc(av_done, 1)

            pe.wait_ge(y_out, UT)
            for c in range(HEADS + 1):
                if c < HEADS:
                    scores(c)
                if c >= 1:
                    turn_att(c - 1)
                if c < HEADS:
                    unit, half = divmod(c, 2)
                    if c == 0:
                        pe.wait_ge(glu_in, 1)
                    if half == 0 and unit >= 2:
                        pe.wait_ge(acc_out, 8 + unit - 1)
                    pe.wait_ge(lo_ready, S_GLU + c + 1)
                    channels_chunk((C_GLU + c) % RING, unit, CK * half, half == 0, half == 1, UT)
                if c >= 1:
                    att_v(c - 1)
            pe.wait_ge(ho_ready, 1)
            for b in range(4):
                for m in range(2):
                    for t in range(TT):
                        last = nc.tensor.transpose(ps[:, 4 + b, T * m + P * t:T * m + P * t + P],
                                                   heads_out[:, TT * (2 * b + m) + t, :], ident[:, :])
                last.then_inc(ho_turned, 1)

            pe.wait_ge(ho_in, 4)
            pe.wait_ge(acc_out, 12)
            pe.wait_ge(z_in, 1)
            for k in range(KT):
                pe.wait_ge(lo_ready, S_OUT + k + 1)
                tokens_chunk((C_OUT + k) % RING, k, k == 0, k == KT - 1)

            pe.wait_ge(xn_ready, 2 * TT)
            for g in range(8):
                if g >= 4:
                    pe.wait_ge(turn_out, 8 + g - 3)
                for kk in range(2):
                    for t in range(TT):
                        k = 2 * g + kk
                        last = nc.tensor.transpose(ps[:, g % 4, T * kk + P * t:T * kk + P * t + P],
                                                   xn2[:, t, P * k:P * k + P], ident[:, :])
                last.then_inc(turn_done, 1)
            pe.wait_ge(turn_out, 16)
            pe.wait_ge(xs_ready, 16)
            with pe.Fori(0, UNITS_FFN) as i:
                for half in (0, 1):
                    if half == 1:
                        pe.wait_ge(taps_done, i * 16 + 1)
                    for q in range(4):
                        pe.wait_ge(lo_ready, i * 8 + (S_UP + 4 * half + q + 1))
                        channels_chunk(q, half, CK * q, q == 0, q == 3, 0)
                pe.wait_ge(taps_done, i * 16 + 9)

            pe.wait_ge(taps_done, 16 * UNITS_FFN + 1)

            def down(i, j, start, stop):
                pe.wait_ge(hs_ready, i * RING + (j + 1))
                pe.wait_ge(lo_ready, i * RING + (S_DOWN + j + 1))
                tokens_chunk(j, j, start, stop)

            for j in range(RING):
                down(0, j, j == 0, False)
            with pe.Fori(1, FT // RING - 1) as i:
                for j in range(RING):
                    down(i, j, False, False)
            for j in range(RING):
                down(FT // RING - 1, j, False, j == RING - 1)


_INS = ['x', 'ln_pre_mix', 'ln_post_mix', 'ln_pre_ffn', 'ln_post_ffn', 'w_in', 'lam_q1', 'lam_k1', 'lam_q2', 'lam_k2',
        'attn_sub_norm', 'rel_bias', 'ssm_a_re', 'ssm_a_im', 'ssm_log_dt', 'ssm_b_re', 'ssm_b_im', 'ssm_c_re',
        'ssm_c_im', 'ssm_d', 'ssm_w_glu', 'w_out', 'w_up', 'conv_w', 'conv_b', 'w_down']


def _bucket_onehot():
    import numpy as np
    table = np.zeros((NB + 1, BAND), np.float32)
    for m in range(BAND):
        dist = T - 1 - m
        if dist < 0:
            b = NB
        elif dist < NB // 2:
            b = dist
        else:
            b = min(NB - 1, NB // 2 + int(math.log(dist / 16) / math.log(128 / 16) * (NB // 2)))
        table[b, m] = 1.0
    return table


def kernel(**inputs):
    import numpy as _np
    import concourse.bacc as _bacc
    from concourse import mybir as _mybir
    from concourse.bass_utils import run_bass_kernel_spmd as _run

    nc = _bacc.Bacc("TRN2", target_bir_lowering=False, num_devices=1, dynamic_dma_scratch_size=1024)
    arrays, args = {}, []
    given = {name: _np.ascontiguousarray(inputs[name]) for name in _INS}
    given["bucket_onehot"] = _bucket_onehot()
    for name, a in given.items():
        arrays[f"in_{name}_dram"] = a
        args.append(nc.dram_tensor(f"in_{name}_dram", a.shape, _mybir.dt.from_np(a.dtype), kind="ExternalInput").ap())
    args.append(nc.dram_tensor("out_0_dram", (1, T, D), F32, kind="ExternalOutput").ap())
    build(nc, *args)
    r = _run(nc, [arrays], core_ids=[0])
    return r.results[0]["out_0_dram"]
```

```python
import math
from contextlib import ExitStack

import concourse.bass as bass
from concourse import mybir

F32 = mybir.dt.float32
F32R = mybir.dt.float32r
ALU = mybir.AluOpType
ACT = mybir.ActivationFunctionType
AX = mybir.AxisListType

P = 128
D = 2048
T = 256
TT = T // P
KT = D // P
D_SSM = D // 2
HEADS = 8
DH = 64
G, HC, PS = 64, 16, 64
NT = G // 2
PAIRS = NT // 2
M = T // 2
UT = D_SSM // P
DFF = 5632
CH = 512
CK = 4
CHUNK = CK * CH
UNITS_FFN = DFF // CH
FT = DFF // P
EPS = 1e-6
NB = 32
BAND = T + P
LAMBDA_INIT = 0.8 - 0.6 * math.exp(-0.3 * 0)
NEG = -1e30

C_QK, C_V, C_GLU, C_OUT, C_UP, C_DOWN = 8, 24, 32, 40, 56, 144
RING = 4
SSM_STEP = 5
V_ORDER = ((0, 2), (0, 3), (1, 2), (1, 3), (0, 0), (0, 1), (1, 0), (1, 1))
OUT_ORDER = tuple(range(UT, KT)) + tuple(range(UT))

MAGIC = 1.5 * 2 ** 23
MAGIC16 = 1.5 * 2 ** 7
INV2PI = 1.0 / (2 * math.pi)
PI_A = 6.28125
PI_B = math.floor((2 * math.pi - PI_A) * 2 ** 19) / 2 ** 19
PI_C = 2 * math.pi - PI_A - PI_B
PI_IN = 3.1415925
HALF_IN = 0.49999997


class Tally:

    def __init__(self, sem):
        self.sem, self.n = sem, 0

    def add(self, ins):
        ins.then_inc(self.sem, 1)
        self.n += 1
        return self.n


def build(nc, x, ln_pre_mix, ln_post_mix, ln_pre_ffn, ln_post_ffn, w_in, lam_q1, lam_k1, lam_q2, lam_k2,
          attn_sub_norm, rel_bias, ssm_a_re, ssm_a_im, ssm_log_dt, ssm_b_re, ssm_b_im, ssm_c_re, ssm_c_im,
          ssm_d, ssm_w_glu, w_out, w_up, conv_w, conv_b, w_down, bucket_onehot, out):
    band_dram = nc.dram_tensor("band_scratch", (HEADS, P, BAND), F32, kind="Internal").ap()

    with ExitStack() as ctx:
        def sb(name, shape, dt=F32):
            return ctx.enter_context(nc.sbuf_tensor(name, shape, dt))

        def sem(name):
            return ctx.enter_context(nc.semaphore(name))

        raw = sb("raw", [P, RING, CHUNK])
        w_hi = sb("w_hi", [P, RING, CHUNK], F32R)
        w_lo = sb("w_lo", [P, RING, CHUNK], F32R)
        xs = sb("xs", [P, KT, 2, T], F32R)
        res = sb("res", [P, TT * D])
        arena = sb("arena", [P, 17408])
        ident = sb("ident", [P, P])
        steps = sb("steps", [P, M])
        consts = sb("consts", [P, 2])
        ones = sb("ones", [1, P])
        warm = sb("warm", [P, 1])
        prm = sb("prm", [P, 3 * NT])
        gain_mix = sb("gain_mix", [P, KT])
        gain_rows = sb("gain_rows", [KT, P])
        prm2 = sb("prm2", [P, UT + 1])
        conv = sb("conv", [P, 4, 2 * FT])
        stat = sb("stat", [P, 4, 5, TT])
        sq4 = sb("sq4", [P, 4])
        heads_stat = sb("heads_stat", [P, 3, HEADS * TT])
        sm = sb("sm", [P, 2, 5, 2, 2])
        ssmp = sb("ssmp", [P, 24, NT])
        lamt = sb("lamt", [1, 4, DH])
        lamj = sb("lamj", [1, DH])
        lams = sb("lams", [1, 6])
        lam_col = sb("lam_col", [P, 1])
        gain_o = sb("gain_o", [P, 1])
        ps = ctx.enter_context(nc.psum_tensor("ps", [P, 8, 512], F32))

        def area(a, n):
            return arena[:, a:a + n]

        x_nat = area(0, 4096).rearrange("p (t d) -> p t d", t=TT)
        qT = area(0, 2048).rearrange("p (m t) -> p m t", t=T)
        kT = area(2048, 2048).rearrange("p (m t) -> p m t", t=T)
        v = area(4096, 2048).rearrange("p (t d) -> p t d", t=TT)
        uT = area(6144, 2048).rearrange("p (m t) -> p m t", t=T)
        zT = uT
        BT = [area(8192 + 1024 * a, 1024).rearrange("p (j q) -> p j q", j=UT) for a in (0, 1)]
        CS = [area(10240 + 1024 * a, 1024).rearrange("p (i e h) -> p i e h", i=NT, e=2) for a in (0, 1)]
        band = area(8192, 3072).rearrange("p (h c) -> p h c", h=HEADS)
        onehot = arena[0:NB + 1, 8192:8192 + BAND]
        bandrow = arena[0:HEADS, 8576:8576 + BAND]
        relb = arena[0:NB + 1, 8960:8960 + HEADS]
        b_diag = [area(4096 + 1024 * a, 1024).rearrange("p (i e h) -> p i e h", i=NT, e=2) for a in (0, 1)]
        c_nat = [area(6144 + 1024 * a, 1024).rearrange("p (j e q) -> p j e q", j=UT, e=2) for a in (0, 1)]
        TMP = 12288
        junk = area(TMP, 2048)
        b_nat = [area(TMP + 2048 + 512 * a, 512).rearrange("p (i h) -> p i h", i=NT) for a in (0, 1)]
        b_prod = [area(TMP + 3072 + 512 * a, 512).rearrange("p (i h) -> p i h", i=NT) for a in (0, 1)]
        rows = area(TMP + 4096, P)
        rows2 = area(TMP + 4224, P)
        ldt2 = area(TMP + 4352, 2)
        rows_conv = area(TMP + 4360, 4 * P).rearrange("p (c n) -> p c n", c=4)
        b_diag2 = [area(1024 * a, 1024).rearrange("p (i e h) -> p i e h", i=NT, e=2) for a in (0, 1)]
        b_prod2 = [area(2048 + 512 * a, 512).rearrange("p (i h) -> p i h", i=NT) for a in (0, 1)]
        cs_prod = [area(3072, 1024), area(TMP + 3072, 1024)]
        BT2 = [res[:, 1024 * a:1024 * a + 1024].rearrange("p (j q) -> p j q", j=UT) for a in (0, 1)]
        CS2 = [res[:, 2048 + 1024 * a:3072 + 1024 * a].rearrange("p (i c) -> p i c", i=NT) for a in (0, 1)]
        tab = [area(TMP + 4 * M * a, 4 * M).rearrange("p (f x) -> p f x", f=2) for a in (0, 1)]
        ph_a = area(TMP + 1024, 2 * M)
        ph_k = area(TMP + 1280, 2 * M)
        ph_f = [area(TMP + 1536 + 2 * M * a, 2 * M) for a in (0, 1)]
        rot_c = area(TMP + 2048, 4 * M).rearrange("p (a x) -> p a x", a=2)
        rot_s = area(TMP + 2560, 4 * M).rearrange("p (a x) -> p a x", a=2)
        scan_in = area(TMP + 3072, 4 * M).rearrange("p (a x) -> p a x", a=2)
        state = [area(TMP + 3584 + 4 * (M + 2) * a, 4 * (M + 2)).rearrange("p (a e m) -> p a e m", a=2, e=2)
                 for a in (0, 1)]
        K0T = area(TMP + 4624, 256).rearrange("p (j h) -> p j h", j=UT)
        sc = [area(TMP + 768 * a, 768).rearrange("p (s c) -> p s c", s=2) for a in (0, 1)]
        att = [area(TMP + 1536 + 384 * a, 384) for a in (0, 1)]
        attT = [area(TMP + 2304 + 384 * a, 384) for a in (0, 1)]
        gate = area(TMP + 3072, 1024).rearrange("p (m t) -> p m t", t=T)
        junk_h = area(TMP + 4096, P)
        heads_out = area(0, 2048).rearrange("p (a c) -> p a c", c=P)
        xn2 = area(0, 4096).rearrange("p (t d) -> p t d", t=TT)
        gain_ffn = area(4096, D)
        hT = area(0, FT * T).rearrange("p (k t) -> p k t", k=FT)
        ca = [area(11264 + 1024 * a, 1024).rearrange("p (m t) -> p m t", m=4) for a in (0, 1)]
        gain = area(13312, D)
        big = area(15360, D)
        pre = [area(15360 + 1024 * a, 1024).rearrange("p (m t) -> p m t", t=T) for a in (0, 1)]
        x1 = res[:, :].rearrange("p (t d) -> p t d", t=TT)

        raw_in = [sem(f"raw_in{j}") for j in range(RING)]
        hi_ready = sem("hi_ready")
        lo_ready = sem("lo_ready")
        split_used = sem("split_used")
        pool_lo = sem("pool_lo")
        x_in = [sem("x_in0"), sem("x_in1")]
        rows_in, rows2_in, conv_in, rel_in = sem("rows_in"), sem("rows2_in"), sem("conv_in"), sem("rel_in")
        lam_in, b_in, c_in = sem("lam_in"), sem("b_in"), sem("c_in")
        band_out, band_in = sem("band_out"), sem("band_in")
        gain0_in, gain0_turned, gain0_ready = sem("gain0_in"), sem("gain0_turned"), sem("gain0_ready")
        res_in, gain1_in, gain_ffn_in, gain2_in = sem("res_in"), sem("gain1_in"), sem("gain_ffn_in"), sem("gain2_in")
        out_done = sem("out_done")
        pool_ready = sem("pool_ready")
        pool_op = sem("pool_op")
        rows_ready = sem("rows_ready")
        sq_done, std_done, rstd_done = sem("sq_done"), sem("std_done"), sem("rstd_done")
        xn_ready = sem("xn_ready")
        turn_done = sem("turn_done")
        xh_ready = sem("xh_ready")
        xs_ready = sem("xs_ready")
        tile_done = sem("tile_done")
        prep_done, prep_out = sem("prep_done"), sem("prep_out")
        par_a, par_v = sem("par_a"), sem("par_v")
        lam_v, lam_a = sem("lam_v"), sem("lam_a")
        bdiag_ready = sem("bdiag_ready")
        f2_ready = sem("f2_ready")
        bdiag2_ready = sem("bdiag2_ready")
        cs2_ready = [sem("cs2_ready0"), sem("cs2_ready1")]
        cs2_step = sem("cs2_step")
        acc_out = sem("acc_out")
        phase_ready = sem("phase_ready")
        tab_abs, tab_ready = sem("tab_abs"), sem("tab_ready")
        bu_done = sem("bu_done")
        bu_used = sem("bu_used")
        tile_op = sem("tile_op")
        zero_ready = sem("zero_ready")
        state_ready = sem("state_ready")
        y_done = sem("y_done")
        y_out = sem("y_out")
        gelu_done = sem("gelu_done")
        glu_hi, glu_in = sem("glu_hi"), sem("glu_in")
        sc_done, sc_read = sem("sc_done"), sem("sc_read")
        sm_op = sem("sm_op")
        neg_ready, exp_done = sem("neg_ready"), sem("exp_done")
        att_ready, att_turned, attT_ready = sem("att_ready"), sem("att_turned"), sem("attT_ready")
        av_done = sem("av_done")
        z_ready, z_hi, z_in = sem("z_ready"), sem("z_hi"), sem("z_in")
        hs_std, hs_rstd, ho_ready, ho_turned = sem("hs_std"), sem("hs_rstd"), sem("ho_ready"), sem("ho_turned")
        ho_hi, ho_in = sem("ho_hi"), sem("ho_in")
        sq4_sum = sem("sq4_sum")
        half_sq = sem("half_sq")
        out_gained = sem("out_gained")
        out_sum = sem("out_sum")
        half_out = sem("half_out")
        merged = sem("merged")
        ca_ready, taps_done, silu_done, h_ready = sem("ca_ready"), sem("taps_done"), sem("silu_done"), sem("h_ready")
        hs_hi, hs_ready = sem("hs_hi"), sem("hs_ready")

        x_d = x[0].rearrange("(t p) d -> t p d", p=P)
        out_d = out[0].rearrange("(t p) d -> t p d", p=P)
        win_d = w_in[0].rearrange("(k p) n -> p k n", p=P)
        wglu_d = ssm_w_glu[0].rearrange("(k p) n -> p k n", p=P)
        wup_d = w_up[0].rearrange("(k p) n -> p k n", p=P)
        wout_d = w_out[0].rearrange("(k p) n -> k p n", p=P)
        wdown_d = w_down[0].rearrange("(k p) n -> p k n", p=P)

        def chunk_source(c):
            if c < C_QK:
                return win_d[:, CK * (c % 4):CK * (c % 4) + CK, 3072 + CH * (c // 4):3072 + CH * (c // 4) + CH]
            if c < C_V:
                u = (c - C_QK) // 4
                return win_d[:, CK * (c % 4):CK * (c % 4) + CK, CH * u:CH * u + CH]
            if c < C_GLU:
                half, quarter = V_ORDER[c - C_V]
                return win_d[:, CK * quarter:CK * quarter + CK, 2048 + CH * half:2048 + CH * half + CH]
            if c < C_OUT:
                u, half = divmod(c - C_GLU, 2)
                return wglu_d[:, CK * half:CK * half + CK, CH * u:CH * u + CH]
            return wout_d[OUT_ORDER[c - C_OUT]]

        def nth(n, t):
            return ((0, 0), (0, 1), (1, 0), (2, 0), (1, 1), (2, 1), (3, 0), (3, 1)).index((n, t)) + 1

        def turned(n, t, b):
            return 8 * n + 4 * t + b + 1

        def taken(n, t, b):
            return 2 * b + t + 1 if n == 0 else turned(n, t, b)

        def group(hi_or_lo, t, b):
            return xs[:, 4 * b:4 * b + 4, hi_or_lo, P * t:P * t + P]

        def turned_ps(n, t, b):
            return ps[:, 2 * b + t if n == 0 else 4 * t + b, :].rearrange("p (k c) -> p k c", c=P)

        def grid(ring, j):
            return ring[:, j, :].rearrange("p (k n) -> p k n", k=CK)

        def acc(unit, m):
            return ps[:, 2 * (unit % 2) + m // 2, T * (m % 2):T * (m % 2) + T]

        def acc_all(unit):
            return ps[:, 2 * (unit % 2):2 * (unit % 2) + 2, :].rearrange("p b (m t) -> p (b m) t", t=T)

        def par(name):
            return ssmp[:, PAR.index(name), :]

        PAR = ["dt", "ad", "th", "k", "r", "rc", "ab", "mag", "cos", "sin", "phi", "phi_h", "phi_l", "lre", "nr",
               "lim", "den", "t1", "t2", "fre", "fim", "f2re", "f2im", "decay"]

        def tile_of(p, e):
            return 8 * (p // 4) + 4 * e + p % 4

        def split_after(p):
            first = lambda n: C_QK + 3 + (0 if n == 0 else 1 + SSM_STEP * (n - 1) // 4)
            return range(first(p), min(first(p + 1), C_V + 6))

        RE_IM = (("re", "im", ALU.subtract), ("im", "re", ALU.add))
        a_re, a_im, log_dt = prm[:, 0:NT], prm[:, NT:2 * NT], prm[:, 2 * NT:3 * NT]

        block = ctx.enter_context(nc.Block())

        @block.sync
        def _(sp):
            def load(dst, src, s):
                sp.dma_start(dst, src).then_inc(s, 16)

            def chunk(c):
                if c >= RING:
                    sp.wait_ge(lo_ready, c - RING + 1)
                dst = grid(raw, c % RING) if c < C_OUT else raw[:, c % RING, :]
                load(dst, chunk_source(c), raw_in[c % RING])

            load(gain_rows[:, :], ln_pre_mix[0].rearrange("(k p) -> k p", p=P), gain0_in)
            for t in range(TT):
                load(x_nat[:, t, :], x_d[t], x_in[t])
            chunk(0)
            load(rows[0:32, :], ssm_a_re[0].rearrange("(i e) p -> i (e p)", e=2), rows_in)
            load(rows[32:64, :], ssm_a_im[0].rearrange("(i e) p -> i (e p)", e=2), rows_in)
            load(ldt2[64:96, :], ssm_log_dt[0].rearrange("(i e) -> i e", e=2), rows_in)
            chunk(1)
            load(rows2[0:8, :], ssm_d[0].rearrange("(k g) h -> k (g h)", k=UT), rows2_in)
            load(rows2[8:9, :], attn_sub_norm[0:1, :], rows2_in)
            load(rows_conv[0:2 * FT, 0:3, :], conv_w[0].rearrange("w o (k p) -> k (w o) p", p=P), conv_in)
            load(rows_conv[0:2 * FT, 3, :], conv_b[0].rearrange("(k p) -> k p", p=P), conv_in)
            load(arena[0:NB, 8960:8960 + HEADS], rel_bias, rel_in)
            load(onehot, bucket_onehot, rel_in)
            chunk(2)
            for n, lv in enumerate((lam_q1, lam_k1, lam_q2, lam_k2)):
                load(lamt[0:1, n, :], lv[0:1, :], lam_in)
            chunk(3)
            for a, cw in enumerate((ssm_c_re, ssm_c_im)):
                for e in (0, 1):
                    load(c_nat[a][:, :, e, :], cw[0].rearrange("g h p -> (g h) p").rearrange("(j r) p -> r j p", r=P),
                         c_in)
            for a, bw in enumerate((ssm_b_re, ssm_b_im)):
                load(b_nat[a], bw[0].rearrange("g p h -> (g p) h").rearrange("(i q) h -> q i h", q=P), b_in)
            for c in range(RING, C_UP):
                chunk(c)
                if c == C_GLU + 4:
                    sp.wait_ge(y_out, UT)
                    for t in range(TT):
                        load(x1[:, t, :], x_d[t], res_in)
                if c == C_OUT + 6:
                    sp.wait_ge(ho_in, 4)
                    load(gain, ln_post_mix[0:1, :].to_broadcast([P, D]), gain1_in)
                    load(gain_ffn, ln_pre_ffn[0:1, :].to_broadcast([P, D]), gain_ffn_in)
            with sp.Fori(0, UNITS_FFN) as i:
                for j in range(8):
                    sp.wait_ge(lo_ready, i * 8 + (C_UP + j - RING + 1))
                    src = wup_d[:, CK * (j % 4):CK * (j % 4) + CK, bass.ds(i * CH + DFF * (j // 4), CH)]
                    sp.dma_start(grid(raw, j % RING), src).then_inc(raw_in[j % RING], 16)
            sp.wait_ge(out_gained, 2 * TT)
            sp.dma_start(gain, ln_post_ffn[0:1, :].to_broadcast([P, D])).then_inc(gain2_in, 16)
            with sp.Fori(0, FT // RING) as i:
                for j in range(RING):
                    sp.wait_ge(lo_ready, i * RING + (C_DOWN + j - RING + 1))
                    sp.dma_start(raw[:, j:j + 1, :], wdown_d[:, bass.ds(i * RING + j, 1), :])\
                        .then_inc(raw_in[j], 16)
            sp.wait_ge(out_sum, 6)
            load(out_d[0], x1[:, 0, :], out_done)
            for q in range(4):
                sp.wait_ge(out_sum, 7 + q)
                load(out_d[1][:, CH * q:CH * q + CH], x1[:, 1, CH * q:CH * q + CH], out_done)
            sp.wait_ge(out_done, 16 * 5)

        @block.gpsimd
        def _(pool):
            k = Tally(pool_ready)
            k.add(nc.gpsimd.memset(ident[:, :], 0.0))
            pool.wait_ge(pool_ready, 1)
            k.add(nc.gpsimd.affine_select(out=ident[:, :], in_=ident[:, :], compare_op=ALU.not_equal, fill=1.0,
                                          base=0, pattern=[[-1, P]], channel_multiplier=1))
            k.add(nc.gpsimd.memset(consts[:, 0:1], EPS))
            k.add(nc.gpsimd.memset(consts[:, 1:2], math.pi / 2))
            k.add(nc.gpsimd.memset(ones[:, :], 1.0))
            pool.wait_ge(pool_ready, 5)
            k.add(nc.gpsimd.memset(arena[NB:NB + 1, 8960:8960 + HEADS], NEG))
            pool.wait_ge(pool_ready, 6)
            k.add(nc.gpsimd.iota(steps[:, :], pattern=[[1, M]], base=0, channel_multiplier=0,
                                 allow_small_or_imprecise_dtypes=True))
            for a in (0, 1):
                k.add(nc.gpsimd.memset(area(4096 + 1024 * a, 1024), 0.0))
            for a in (0, 1):
                k.add(nc.gpsimd.memset(area(10240 + 1024 * a, 1024), 0.0))
            top = Tally(pool_op)

            def step(ins):
                pool.wait_ge(pool_op, top.add(ins))

            pool.wait_ge(turn_done, 8)
            step(nc.gpsimd.memset(area(0, 2048), 0.0))
            pool.wait_ge(f2_ready, 1)
            pool.wait_ge(b_in, 32)
            for a, (f0, f1, op) in enumerate(RE_IM):
                for n, f in enumerate((f0, f1)):
                    step(nc.gpsimd.tensor_tensor(b_prod2[n], b_nat[n],
                                                 par("f2" + f).unsqueeze(2).to_broadcast([P, NT, HC]), ALU.mult))
                for e in (0, 1):
                    half = slice(PS * e, PS * e + PS)
                    nc.gpsimd.tensor_tensor(b_diag2[a][half, :, e, :], b_prod2[0][half], b_prod2[1][half], op)\
                        .then_inc(bdiag2_ready, 1)
                    pool.wait_ge(bdiag2_ready, 2 * a + e + 1)

            def phases(p):
                def times(dst, name):
                    both = par(name)[:, tile_of(p, 0):tile_of(p, 1) + 1:4]
                    step(nc.gpsimd.tensor_tensor(dst.rearrange("p (e m) -> p e m", e=2),
                                                 steps[:, :].unsqueeze(1).to_broadcast([P, 2, M]),
                                                 both.unsqueeze(2).to_broadcast([P, 2, M]), ALU.mult))
                f = ph_f[p % 2]
                times(ph_a, "phi_h")
                times(ph_k, "phi")
                step(nc.gpsimd.tensor_scalar(ph_k, ph_k, MAGIC, MAGIC, ALU.add, ALU.subtract))
                step(nc.gpsimd.tensor_tensor(ph_a, ph_a, ph_k, ALU.subtract))
                times(ph_k, "phi_l")
                if p >= 2:
                    pool.wait_ge(tab_ready, p - 1)
                step(nc.gpsimd.tensor_tensor(f, ph_a, ph_k, ALU.add))
                nc.gpsimd.tensor_scalar(f, f, HALF_IN, -HALF_IN, ALU.min, ALU.max).then_inc(phase_ready, 1)

            phases(0)
            pool.wait_ge(prep_out, 8)
            lam_of = lambda name: par(name).unsqueeze(2).to_broadcast([P, NT, 2 * HC])
            flat = lambda m: m.rearrange("p i e h -> p i (e h)")
            prod = cs_prod[0].rearrange("p (i c) -> p i c", i=NT)
            step(nc.gpsimd.tensor_tensor(CS2[0], flat(CS[0]), lam_of("lre"), ALU.mult))
            step(nc.gpsimd.tensor_tensor(prod, flat(CS[1]), lam_of("lim"), ALU.mult))
            nc.gpsimd.tensor_tensor(CS2[0], CS2[0], prod, ALU.add).then_inc(cs2_ready[0], 1)
            pool.wait_ge(bdiag_ready, 4)
            pool.wait_ge(prep_out, 14)
            pool.wait_ge(cs2_ready[1], 1)
            for a in (0, 1):
                nc.gpsimd.memset(area(TMP + 3584 + 4 * (M + 2) * a, 4 * (M + 2)), 0.0).then_inc(zero_ready, 1)
            for p in range(1, PAIRS):
                phases(p)
            for s in range(C_UP + 1, C_UP + RING):
                j = s % RING
                pool.wait_ge(hi_ready, s + 1)
                nc.gpsimd.tensor_tensor(w_lo[:, j, :], raw[:, j, :], w_hi[:, j, :].bitcast(F32), ALU.subtract)\
                    .then_inc(pool_lo, 1)

        @block.scalar
        def _(act):
            def norm(n, t, src, scratch):
                act.wait_ge(sq_done, nth(n, t) - 1)
                nc.scalar.activation(scratch, src, ACT.Square, accum_out=stat[:, n, 0, t:t + 1]).then_inc(sq_done, 1)
                act.wait_ge(sq_done, nth(n, t))
                nc.scalar.activation(stat[:, n, 1, t:t + 1], stat[:, n, 0, t:t + 1], ACT.Sqrt, bias=consts[:, 0:1],
                                     scale=1.0 / D).then_inc(std_done, 1)

            def norm_ps(n, t):
                m = n // 2 * TT + t
                if (n, t) == (1, 1):
                    act.wait_ge(split_used, C_UP)
                else:
                    act.wait_ge(tile_done, 1 if n == 1 else t + 2)
                halves = [ps[:, 4 * t + 2 * b:4 * t + 2 * b + 2, :].rearrange("p b n -> p (b n)") for b in (0, 1)]
                nc.scalar.activation(big[:, 0:D // 2], halves[0], ACT.Square, accum_out=stat[:, n, 0, t:t + 1])\
                    .then_inc(half_sq, 1)
                act.wait_ge(half_sq, 2 * m + 1)
                nc.scalar.activation(stat[:, n, 4, t:t + 1], stat[:, n, 0, t:t + 1], ACT.Identity,
                                     bias=consts[:, 0:1], scale=1.0 / D).then_inc(sq_done, 1)
                act.wait_ge(out_gained, 2 * m + 1)
                nc.scalar.activation(big[:, D // 2:D], halves[1], ACT.Square, accum_out=stat[:, n, 3, t:t + 1])\
                    .then_inc(half_sq, 1)
                act.wait_ge(sq_done, nth(n, t))
                act.wait_ge(half_sq, 2 * m + 2)
                nc.scalar.activation(stat[:, n, 1, t:t + 1], stat[:, n, 3, t:t + 1], ACT.Sqrt,
                                     bias=stat[:, n, 4, t:t + 1], scale=1.0 / D).then_inc(std_done, 1)

            def take_hi(n, t, b):
                act.wait_ge(turn_done, turned(n, t, b))
                if n == 0:
                    for kk in range(4):
                        k = 4 * b + kk
                        last = nc.scalar.activation(xs[:, k, 0, P * t:P * t + P], turned_ps(0, t, b)[:, kk, :],
                                                    ACT.Identity, scale=gain_mix[:, k:k + 1])
                else:
                    last = nc.scalar.copy(group(0, t, b), turned_ps(1, t, b))
                last.then_inc(xh_ready, 1)

            def hi(c):
                act.wait_ge(raw_in[c % RING], 16 * (c // RING + 1))
                if c >= RING:
                    act.wait_ge(split_used, c - RING + 1)
                nc.scalar.copy(w_hi[:, c % RING, :], raw[:, c % RING, :]).then_inc(hi_ready, 1)

            def prep(n):
                act.wait_ge(prep_done, n + 1)
                return ps[:, 4 + n % 4, :]

            act.wait_ge(pool_ready, 4)
            nc.scalar.activation(warm[:, :], consts[:, 0:1], ACT.Sqrt).then_inc(par_a, 1)
            act.wait_ge(gain0_turned, 1)
            nc.scalar.copy(gain_mix[:, :], ps[:, 7, 0:KT]).then_inc(gain0_ready, 1)
            for t in range(TT):
                act.wait_ge(x_in[t], 16)
                norm(0, t, x_nat[:, t, :], junk)
            act.wait_ge(gain0_ready, 1)
            take_hi(0, 0, 0)
            hi(0)
            take_hi(0, 1, 0)
            for b in range(1, 4):
                take_hi(0, 0, b)
                take_hi(0, 1, b)
                hi(b)
            nc.scalar.copy(prm[:, :], prep(0)[:, 0:3 * NT]).then_inc(prep_out, 1)
            act.wait_ge(prep_out, 1)
            nc.scalar.activation(par("dt"), log_dt, ACT.Exp).then_inc(par_a, 1)
            hi(4)
            act.wait_ge(par_v, 1)
            nc.scalar.activation(par("mag"), par("ad"), ACT.Exp).then_inc(par_a, 1)
            act.wait_ge(lam_v, 2)
            nc.scalar.activation(lams[:, 2:4], lams[:, 0:2], ACT.Exp).then_inc(lam_a, 1)
            act.wait_ge(par_v, 9)
            nc.scalar.activation(par("sin"), par("rc"), ACT.Sin).then_inc(par_a, 1)
            nc.scalar.activation(par("cos"), par("ab"), ACT.Sin, bias=consts[:, 1:2], scale=-1.0).then_inc(par_a, 1)
            nc.scalar.copy(prm2[:, :], prep(1)[:, 0:UT + 1]).then_inc(prep_out, 1)
            nc.scalar.copy(conv[:, :, :], prep(2)[:, 0:8 * FT].rearrange("p (c k) -> p c k", c=4)).then_inc(prep_out, 1)
            nc.scalar.copy(bandrow, prep(3)[0:HEADS, 0:BAND]).then_inc(prep_out, 1)
            act.wait_ge(prep_out, 4)
            act.dma_start(band_dram, bandrow.unsqueeze(1).to_broadcast([HEADS, P, BAND])).then_inc(band_out, 16)
            for a in (0, 1):
                for q in (0, 1):
                    src = prep(4 + 2 * a + q).rearrange("p (i e h) -> p i e h", e=2, h=HC)
                    for e in (0, 1):
                        half = slice(PS * e, PS * e + PS)
                        last = nc.scalar.activation(CS[a][half, 16 * q:16 * q + 16, e, :], src[half, :, e, :],
                                                    ACT.Identity, scale=1.0 - 2.0 * a)
                    last.then_inc(prep_out, 1)
            for c in range(5, 8):
                hi(c)

            def take_u(u):
                act.wait_ge(split_used, 4 * (u + 1))
                nc.scalar.copy(uT[:, 4 * u:4 * u + 4, :], acc_all(u)).then_inc(acc_out, 1)

            take_u(0)
            hi(8)
            nc.scalar.copy(lam_col[:, :], prep(8)[:, 0:1]).then_inc(prep_out, 1)
            act.wait_ge(band_out, 16)
            for n, dst in ((9, BT[0]), (11, BT[1]), (14, BT2[0]), (16, BT2[1])):
                for q in (0, 1):
                    nc.scalar.copy(dst[:, 4 * q:4 * q + 4, :],
                                   prep(n + q).rearrange("p (j q) -> p j q", j=4)).then_inc(prep_out, 1)
                if n == 11:
                    nc.scalar.copy(K0T, prep(13)[:, 0:256].rearrange("p (j h) -> p j h", j=UT)).then_inc(prep_out, 1)
                    hi(9)
            hi(10)
            take_u(1)

            def table(p):
                act.wait_ge(phase_ready, p + 1)
                if p >= 2:
                    act.wait_ge(state_ready, 2 * p - 2)
                nc.scalar.activation(tab[p % 2][:, 0, :], ph_f[p % 2], ACT.Abs).then_inc(tab_abs, 1)
                nc.scalar.activation(tab[p % 2][:, 1, :], ph_f[p % 2], ACT.Sin, scale=2 * math.pi)
                act.wait_ge(tab_abs, p + 1)
                nc.scalar.activation(tab[p % 2][:, 0, :], tab[p % 2][:, 0, :], ACT.Sin, bias=consts[:, 1:2],
                                     scale=-2 * math.pi).then_inc(tab_ready, 1)

            def take_qk(u):
                act.wait_ge(split_used, C_QK + 4 * (u + 1))
                dst = (qT if u < 2 else kT)[:, 4 * (u % 2):4 * (u % 2) + 4, :]
                nc.scalar.copy(dst, acc_all(u)).then_inc(acc_out, 1)

            def take_v(half):
                act.wait_ge(split_used, C_V + 6 + 2 * half)
                nc.scalar.copy(v[:, :, CH * half:CH * half + CH], ps[:, 2 * half:2 * half + 2, :])\
                    .then_inc(acc_out, 1)

            table(0)
            table(1)
            for p in range(PAIRS):
                for c in split_after(p):
                    hi(c)
                    if (c - C_QK) % 4 == 3 and C_QK + 4 < c < C_V + 4:
                        if c == C_QK + 7:
                            act.wait_ge(cs2_ready[0], 1)
                        take_qk((c - C_QK) // 4 - 1)
                if p + 2 < PAIRS:
                    table(p + 2)
            for c in range(C_V + 6, C_GLU + 1):
                hi(c)
            act.wait_ge(y_out, UT)
            shifted = lambda m, n: bass.AP(band_dram.tensor, P - 1 + m, [[BAND - 1, P], [P * BAND, HEADS], [1, n]])
            act.dma_start(band[:, :, 0:P], shifted(P, P)).then_inc(band_in, 16)
            act.dma_start(band[:, :, P:P + T], shifted(0, T)).then_inc(band_in, 16)
            nc.scalar.activation(uT, uT, ACT.Gelu_apprx_tanh).then_inc(gelu_done, 1)
            act.wait_ge(gelu_done, 1)
            act.wait_ge(split_used, C_V + 4)
            nc.scalar.copy(xs[:, UT:KT, 0, :], uT).then_inc(glu_hi, 1)
            hi(C_GLU + 1)
            take_v(0)

            def take_attT(h):
                act.wait_ge(att_turned, h + 1)
                if h >= 2:
                    act.wait_ge(av_done, h - 1)
                nc.scalar.copy(attT[h % 2], ps[:, 6, 0:384]).then_inc(attT_ready, 1)

            def take_head(h):
                act.wait_ge(av_done, h + 1)
                nc.scalar.copy(heads_out[:, TT * h:TT * h + TT, :],
                               ps[:, 7, 0:T].rearrange("p (t c) -> p t c", t=TT))
                for t in range(TT):
                    act.wait_ge(hs_std, TT * h + t)
                    nc.scalar.activation(junk_h, ps[:, 7, P * t:P * t + P], ACT.Square,
                                         accum_out=heads_stat[:, 0, TT * h + t:TT * h + t + 1]).then_inc(hs_std, 1)

            def exps(c):
                act.wait_ge(neg_ready, c + 1)
                for s in (0, 1):
                    for t, cols in ((0, slice(0, P)), (1, slice(P, P + T))):
                        last = nc.scalar.activation(sc[c % 2][:, s, cols], sc[c % 2][:, s, cols], ACT.Exp,
                                                    bias=sm[:, c % 2, 1, t, s:s + 1],
                                                    accum_out=sm[:, c % 2, 2, t, s:s + 1])
                last.then_inc(exp_done, 1)

            exps(0)
            hi(C_GLU + 2)
            take_v(1)
            for c in range(HEADS):
                if c + 1 < HEADS:
                    exps(c + 1)
                take_attT(c)
                hi(C_GLU + 3 + c)
                if c == HEADS - 1:
                    act.wait_ge(z_ready, 1)
                    act.wait_ge(split_used, C_GLU + HEADS - 1)
                    nc.scalar.copy(xs[:, UT:UT + 4, 0, :], zT[:, 0:4, :]).then_inc(z_hi, 1)
                if c % 2:
                    u = c // 2
                    act.wait_ge(split_used, C_GLU + c + 1)
                    if u < 2:
                        nc.scalar.copy(zT[:, 4 * u:4 * u + 4, :], acc_all(u)).then_inc(acc_out, 1)
                    else:
                        if u == 3:
                            act.wait_ge(z_ready, 1)
                        nc.scalar.activation(gate, acc_all(u), ACT.Sigmoid).then_inc(acc_out, 1)
                take_head(c)
            act.wait_ge(hs_std, HEADS * TT)
            nc.scalar.activation(heads_stat[:, 1, :], heads_stat[:, 0, :], ACT.Sqrt, bias=consts[:, 0:1],
                                 scale=1.0 / P).then_inc(hs_std, 1)
            hi(C_OUT + 3)
            act.wait_ge(z_ready, 2)
            nc.scalar.copy(xs[:, UT + 4:KT, 0, :], zT[:, 4:8, :]).then_inc(z_hi, 1)
            for b in range(4):
                act.wait_ge(ho_turned, b + 1)
                nc.scalar.activation(xs[:, 2 * b:2 * b + 2, 0, :], ps[:, 4 + b, :].rearrange("p (m t) -> p m t", t=T),
                                     ACT.Identity, scale=gain_o[:, 0:1]).then_inc(ho_hi, 1)
            for s in range(C_OUT + RING, C_UP):
                hi(s)

            norm_ps(1, 0)
            hi(C_UP)
            act.wait_ge(out_sum, 1)
            norm(2, 0, x1[:, 0, :], big)
            hi(C_UP + 1)
            norm_ps(1, 1)
            take_hi(1, 0, 0)
            take_hi(1, 0, 1)
            for b in range(4):
                act.wait_ge(out_sum, 2 + b)
                cols = slice(CH * b, CH * b + CH)
                last = nc.scalar.activation(big[:, cols], x1[:, 1, cols], ACT.Square, accum_out=sq4[:, b:b + 1])
            last.then_inc(sq_done, 1)
            take_hi(1, 0, 2)
            act.wait_ge(sq4_sum, 1)
            nc.scalar.activation(stat[:, 2, 1, 1:2], stat[:, 2, 0, 1:2], ACT.Sqrt, bias=consts[:, 0:1],
                                 scale=1.0 / D).then_inc(std_done, 1)
            take_hi(1, 0, 3)
            for b in range(4):
                take_hi(1, 1, b)
            hi(C_UP + 2)
            hi(C_UP + 3)

            def hi_loop(j, s, loads):
                act.wait_ge(raw_in[j], loads)
                act.wait_ge(split_used, s)
                nc.scalar.copy(w_hi[:, j, :], raw[:, j, :]).then_inc(hi_ready, 1)

            def first_tap(i, a):
                act.wait_ge(split_used, i * 8 + (C_UP + 4 * a + 4))
                if a == 0:
                    act.wait_ge(h_ready, i + 1)
                for b in (0, 1):
                    nc.scalar.copy(pre[a][:, 2 * b:2 * b + 2, :], ps[:, 4 * a + 2 * b:4 * a + 2 * b + 2, T:2 * T])\
                        .then_inc(half_out, 1)
                for m in range(4):
                    if m % 2 == 0:
                        act.wait_ge(merged, i * 4 + (2 * a + m // 2 + 1))
                    col = i * 4 + (m + FT * a)
                    last = nc.scalar.activation(ca[a][:, m, :], pre[a][:, m, :], ACT.Identity,
                                                scale=conv[:, 2, bass.ds(col, 1)], bias=conv[:, 3, bass.ds(col, 1)])
                    if m % 2:
                        last.then_inc(ca_ready, 1)

            def unit(i, last):
                for j in range(RING):
                    hi_loop(j, i * 8 + (C_UP + j + 1), i * 32 + 16 * (C_UP // RING + 2))
                first_tap(i, 0)
                for j in range(RING):
                    hi_loop(j, i * 8 + (C_UP + RING + j + 1), i * 32 + 16 * (C_UP // RING + 3))
                    if last and j == 0:
                        nc.scalar.copy(xs[:, 0:RING, 0, :], hT[:, 0:RING, :]).then_inc(hs_hi, RING)
                first_tap(i, 1)
                act.wait_ge(taps_done, i * 16 + 9)
                nc.scalar.activation(ca[0], ca[0], ACT.Silu).then_inc(silu_done, 1)

            with act.Fori(0, UNITS_FFN - 1) as i:
                unit(i, False)
            unit(UNITS_FFN - 1, True)
            nc.scalar.activation(warm[:, :], consts[:, 0:1], ACT.Sqrt)

            def hidden_hi(j, k):
                nc.scalar.copy(xs[:, j:j + 1, 0, :], hT[:, k, :]).then_inc(hs_hi, 1)

            act.wait_ge(h_ready, UNITS_FFN + 1)
            with act.Fori(0, FT // RING - 1) as i:
                for j in range(RING):
                    hi_loop(j, i * RING + (C_DOWN + j + 1), i * 16 + 16 * (C_UP // RING + 22 + 2))
                    hidden_hi(j, bass.ds(i * RING + (RING + j), 1))
            for t in range(TT):
                norm_ps(3, t)

        @block.vector
        def _(dve):
            V = nc.vector

            def rstd(n, t):
                dve.wait_ge(std_done, nth(n, t))
                V.reciprocal(stat[:, n, 2, t:t + 1], stat[:, n, 1, t:t + 1]).then_inc(rstd_done, 1)
                dve.wait_ge(rstd_done, nth(n, t))

            def take_lo(n, t, b):
                dve.wait_ge(xh_ready, taken(n, t, b))
                if n == 0:
                    for kk in range(4):
                        k = 4 * b + kk
                        cols = slice(P * t, P * t + P)
                        last = V.scalar_tensor_tensor(xs[:, k, 1, cols], turned_ps(0, t, b)[:, kk, :],
                                                      gain_mix[:, k:k + 1], xs[:, k, 0, cols].bitcast(F32),
                                                      ALU.mult, ALU.subtract)
                else:
                    last = V.tensor_tensor(group(1, t, b), turned_ps(1, t, b), group(0, t, b).bitcast(F32),
                                           ALU.subtract)
                last.then_inc(xs_ready, 1)

            def lo(c):
                j = c % RING
                dve.wait_ge(hi_ready, c + 1)
                V.tensor_tensor(w_lo[:, j, :], raw[:, j, :], w_hi[:, j, :].bitcast(F32), ALU.subtract)\
                    .then_inc(lo_ready, 1)

            for t in range(TT):
                rstd(0, t)
                V.tensor_scalar(x_nat[:, t, :], x_nat[:, t, :], stat[:, 0, 2, t:t + 1], None, ALU.mult)\
                    .then_inc(xn_ready, 1)
            dve.wait_ge(gain0_ready, 1)
            take_lo(0, 0, 0)
            lo(0)
            take_lo(0, 1, 0)
            dve.wait_ge(rows_in, 16 * 3)
            V.tensor_copy(rows[64:96, :].rearrange("p (e q) -> p e q", e=2),
                          ldt2[64:96, :].unsqueeze(2).to_broadcast([32, 2, PS])).then_inc(rows_ready, 1)
            for b in range(1, 4):
                take_lo(0, 0, b)
                take_lo(0, 1, b)
                lo(b)

            lv = Tally(lam_v)
            dve.wait_ge(lam_in, 16 * 4)
            for n in (0, 1):
                if n:
                    dve.wait_ge(lam_v, 1)
                lv.add(V.tensor_tensor_reduce(out=lamj[:, :], in0=lamt[0:1, 2 * n, :], in1=lamt[0:1, 2 * n + 1, :],
                                              scale=1.0, scalar=0.0, op0=ALU.mult, op1=ALU.add,
                                              accum_out=lams[0:1, n:n + 1]))
            pv = Tally(par_v)

            def step(ins):
                dve.wait_ge(par_v, pv.add(ins))

            dve.wait_ge(par_a, 2)
            step(V.tensor_tensor(par("ad"), a_re, par("dt"), ALU.mult))
            step(V.tensor_tensor(par("th"), a_im, par("dt"), ALU.mult))
            step(V.tensor_scalar(par("k"), par("th"), INV2PI, MAGIC, ALU.mult, ALU.add))
            step(V.tensor_scalar(par("k"), par("k"), MAGIC, None, ALU.subtract))
            for n, part in enumerate((PI_A, PI_B, PI_C)):
                step(V.scalar_tensor_tensor(par("r"), par("k"), -part, par("th" if n == 0 else "r"),
                                            ALU.mult, ALU.add))
            step(V.tensor_scalar(par("rc"), par("r"), PI_IN, -PI_IN, ALU.min, ALU.max))
            step(V.scalar_tensor_tensor(par("ab"), par("rc"), -1.0, par("rc"), ALU.mult, ALU.max))
            step(V.tensor_scalar(par("r"), par("r"), 2.0, None, ALU.mult))
            step(V.tensor_scalar(par("phi"), par("r"), INV2PI, None, ALU.mult))
            step(V.tensor_scalar(par("phi_h"), par("phi"), MAGIC16, MAGIC16, ALU.add, ALU.subtract))
            for n, part in enumerate((PI_A, PI_B, PI_C)):
                step(V.scalar_tensor_tensor(par("phi_l"), par("phi_h"), -part, par("r" if n == 0 else "phi_l"),
                                            ALU.mult, ALU.add))
            step(V.tensor_scalar(par("phi_l"), par("phi_l"), INV2PI, None, ALU.mult))
            step(V.tensor_tensor(par("den"), a_re, a_re, ALU.mult))
            step(V.tensor_tensor(par("t1"), a_im, a_im, ALU.mult))
            step(V.tensor_tensor(par("den"), par("den"), par("t1"), ALU.add))
            step(V.reciprocal(par("den"), par("den")))
            lo(4)
            dve.wait_ge(par_a, 5)
            step(V.tensor_tensor(par("lre"), par("mag"), par("cos"), ALU.mult))
            step(V.tensor_scalar(par("nr"), par("lre"), 1.0, None, ALU.subtract))
            step(V.tensor_tensor(par("lim"), par("mag"), par("sin"), ALU.mult))
            step(V.tensor_tensor(par("decay"), par("mag"), par("mag"), ALU.mult))

            def complex_product(dst_re, dst_im, x_re, x_im, y_re, y_im):
                step(V.tensor_tensor(par("t1"), x_re, y_re, ALU.mult))
                step(V.tensor_tensor(par("t2"), x_im, y_im, ALU.mult))
                step(V.tensor_tensor(dst_re, par("t1"), par("t2"), ALU.subtract))
                step(V.tensor_tensor(par("t1"), x_re, y_im, ALU.mult))
                step(V.tensor_tensor(par("t2"), x_im, y_re, ALU.mult))
                step(V.tensor_tensor(dst_im, par("t1"), par("t2"), ALU.add))

            step(V.tensor_tensor(par("t1"), par("nr"), a_re, ALU.mult))
            step(V.tensor_tensor(par("t2"), par("lim"), a_im, ALU.mult))
            step(V.tensor_tensor(par("t1"), par("t1"), par("t2"), ALU.add))
            step(V.tensor_tensor(par("fre"), par("t1"), par("den"), ALU.mult))
            step(V.tensor_tensor(par("t1"), par("lim"), a_re, ALU.mult))
            step(V.tensor_tensor(par("t2"), par("nr"), a_im, ALU.mult))
            step(V.tensor_tensor(par("t1"), par("t1"), par("t2"), ALU.subtract))
            step(V.tensor_tensor(par("fim"), par("t1"), par("den"), ALU.mult))
            complex_product(par("f2re"), par("f2im"), par("lre"), par("lim"), par("fre"), par("fim"))
            dve.sem_inc(f2_ready, 1)
            lo(5)
            dve.wait_ge(b_in, 32)
            dve.wait_ge(pool_ready, 11)
            for a, (f0, f1, op) in enumerate(RE_IM):
                for n, f in enumerate((f0, f1)):
                    step(V.tensor_tensor(b_prod[n], b_nat[n], par("f" + f).unsqueeze(2).to_broadcast([P, NT, HC]),
                                         ALU.mult))
                for e in (0, 1):
                    half = slice(PS * e, PS * e + PS)
                    V.tensor_tensor(b_diag[a][half, :, e, :], b_prod[0][half], b_prod[1][half], op)\
                        .then_inc(bdiag_ready, 1)
                dve.wait_ge(bdiag_ready, 2 * a + 2)
            dve.wait_ge(lam_a, 1)
            lv.add(V.tensor_tensor(lams[:, 4:5], lams[:, 2:3], lams[:, 3:4], ALU.subtract))
            dve.wait_ge(lam_v, 3)
            lv.add(V.tensor_scalar(lams[:, 5:6], lams[:, 4:5], LAMBDA_INIT, -1.0, ALU.add, ALU.mult))
            lo(6)
            lo(7)
            dve.wait_ge(prep_out, 8)
            V.tensor_scalar(gain_o[:, :], prm2[:, UT:UT + 1], 1.0 - LAMBDA_INIT, None, ALU.mult)
            lam_of = lambda name: par(name).unsqueeze(2).to_broadcast([P, NT, 2 * HC])
            flat = lambda m: m.rearrange("p i e h -> p i (e h)")
            prod = cs_prod[1].rearrange("p (i c) -> p i c", i=NT)
            V.tensor_tensor(CS2[1], flat(CS[1]), lam_of("lre"), ALU.mult).then_inc(cs2_step, 1)
            V.tensor_tensor(prod, flat(CS[0]), lam_of("lim"), ALU.mult).then_inc(cs2_step, 1)
            dve.wait_ge(cs2_step, 2)
            V.tensor_tensor(CS2[1], CS2[1], prod, ALU.subtract).then_inc(cs2_ready[1], 1)
            for c in range(C_QK, C_QK + 3):
                lo(c)

            def add_skip(g):
                dve.wait_ge(y_done, 4 * g + 4)
                for e in (0, 1):
                    j = 2 * g + e
                    u = uT[:, j, :].rearrange("p (m o) -> p o m", o=2)
                    V.scalar_tensor_tensor(u, u, prm2[:, j:j + 1],
                                           ps[:, 6 + g % 2, T * e:T * e + T].rearrange("p (o m) -> p o m", o=2),
                                           ALU.mult, ALU.add).then_inc(y_out, 1)

            top = Tally(tile_op)
            dve.wait_ge(zero_ready, 2)
            for p in range(PAIRS):
                bu = ps[:, 4 + p % 2, :].rearrange("p (a x) -> p a x", a=2)
                cos2 = tab[p % 2][:, 0:1, :].to_broadcast([P, 2, 2 * M])
                sin2 = tab[p % 2][:, 1:2, :].to_broadcast([P, 2, 2 * M])
                dve.wait_ge(tab_ready, p + 1)
                dve.wait_ge(bu_done, p + 1)
                top.add(V.tensor_tensor(rot_c, bu, cos2, ALU.mult))
                V.tensor_tensor(rot_s, bu, sin2, ALU.mult).then_inc(bu_used, 1)
                dve.wait_ge(tile_op, top.n)
                dve.wait_ge(bu_used, p + 1)
                top.add(V.tensor_tensor(scan_in[:, 0, :], rot_c[:, 0, :], rot_s[:, 1, :], ALU.add))
                top.add(V.tensor_tensor(scan_in[:, 1, :], rot_c[:, 1, :], rot_s[:, 0, :], ALU.subtract))
                dve.wait_ge(tile_op, top.n)
                for a in (0, 1):
                    for e in (0, 1):
                        tile = slice(M * e, M * e + M)
                        i = tile_of(p, e)
                        decay = par("decay")[:, i:i + 1].to_broadcast([P, M])
                        top.add(V.tensor_tensor_scan(rot_c[:, a, tile], decay, scan_in[:, a, tile], 0.0,
                                                     ALU.mult, ALU.add))
                dve.wait_ge(tile_op, top.n)
                top.add(V.tensor_tensor(scan_in, rot_c, cos2, ALU.mult))
                top.add(V.tensor_tensor(rot_s, rot_c, sin2, ALU.mult))
                dve.wait_ge(tile_op, top.n)
                if p >= 2:
                    dve.wait_ge(y_done, p - 1)
                for a, op in ((0, ALU.subtract), (1, ALU.add)):
                    V.tensor_tensor(state[p % 2][:, a, :, 1:M + 1],
                                    scan_in[:, a, :].rearrange("p (e m) -> p e m", e=2),
                                    rot_s[:, 1 - a, :].rearrange("p (e m) -> p e m", e=2), op)\
                        .then_inc(state_ready, 1)
                dve.wait_ge(state_ready, 2 * p + 2)
                for c in split_after(p):
                    lo(c)
                if p % 4 == 1 and p > 1:
                    add_skip(p // 4 - 1)
            lo(C_V + 6)
            add_skip(PAIRS // 4 - 1)
            lo(C_V + 7)
            lo(C_GLU)
            dve.wait_ge(glu_hi, 1)
            V.tensor_tensor(xs[:, UT:KT, 1, :], uT, xs[:, UT:KT, 0, :].bitcast(F32), ALU.subtract).then_inc(glu_in, 1)

            so = Tally(sm_op)
            TILES = ((0, slice(0, P)), (1, slice(P, P + T)))
            dve.wait_ge(band_in, 32)
            dve.wait_ge(prep_out, 9)

            def biased(h):
                e, st = sc[h % 2], sm[:, h % 2]
                dve.wait_ge(sc_done, h + 1)
                for s in (0, 1):
                    V.scalar_tensor_tensor(e[:, s, :], ps[:, 4 + s, 0:384], DH ** -0.5, band[:, h, :],
                                           ALU.mult, ALU.add).then_inc(sc_read, 1)
                dve.wait_ge(sc_read, 2 * h + 2)
                for t, cols in TILES:
                    so.add(V.tensor_reduce(st[:, 0, t, :], e[:, :, cols], AX.X, ALU.max))
                dve.wait_ge(sm_op, so.n)
                V.tensor_scalar(st[:, 1, :, :], st[:, 0, :, :], -1.0, None, ALU.mult).then_inc(neg_ready, 1)

            def difference(h):
                e, st = sc[h % 2], sm[:, h % 2]
                dve.wait_ge(exp_done, h + 1)
                so.add(V.reciprocal(st[:, 3, :, :], st[:, 2, :, :]))
                dve.wait_ge(sm_op, so.n)
                so.add(V.tensor_scalar(st[:, 4, :, :], st[:, 3, :, :], lam_col[:, 0:1], None, ALU.mult))
                dve.wait_ge(sm_op, so.n)
                for t, cols in TILES:
                    so.add(V.tensor_scalar(e[:, 1, cols], e[:, 1, cols], st[:, 4, t, 1:2], None, ALU.mult))
                dve.wait_ge(sm_op, so.n)
                if h >= 2:
                    dve.wait_ge(att_turned, h - 1)
                for t, cols in TILES:
                    V.scalar_tensor_tensor(att[h % 2][:, cols], e[:, 0, cols], st[:, 3, t, 0:1], e[:, 1, cols],
                                           ALU.mult, ALU.add).then_inc(att_ready, 1)

            def gated(u):
                dve.wait_ge(acc_out, 8 + 2 + u + 1)
                V.tensor_tensor(zT[:, 4 * u:4 * u + 4, :], zT[:, 4 * u:4 * u + 4, :], gate, ALU.mult)\
                    .then_inc(z_ready, 1)

            def gated_lo(u):
                dve.wait_ge(z_hi, u + 1)
                V.tensor_tensor(xs[:, UT + 4 * u:UT + 4 * u + 4, 1, :], zT[:, 4 * u:4 * u + 4, :],
                                xs[:, UT + 4 * u:UT + 4 * u + 4, 0, :].bitcast(F32), ALU.subtract).then_inc(z_in, 1)

            biased(0)
            lo(C_GLU + 1)
            difference(0)
            for c in range(HEADS):
                if c + 1 < HEADS:
                    biased(c + 1)
                lo(C_GLU + 2 + c)
                if c + 1 < HEADS:
                    difference(c + 1)
                if c == HEADS - 2:
                    gated(0)
            gated_lo(0)
            lo(C_OUT + 2)
            dve.wait_ge(hs_std, HEADS * TT + 1)
            V.reciprocal(heads_stat[:, 2, :], heads_stat[:, 1, :]).then_inc(hs_rstd, 1)
            dve.wait_ge(hs_rstd, 1)
            V.tensor_tensor(heads_out, heads_out, heads_stat[:, 2, :].unsqueeze(2).to_broadcast([P, HEADS * TT, P]),
                            ALU.mult).then_inc(ho_ready, 1)
            lo(C_OUT + 3)
            gated(1)
            for b in range(4):
                dve.wait_ge(ho_hi, b + 1)
                V.scalar_tensor_tensor(xs[:, 2 * b:2 * b + 2, 1, :], ps[:, 4 + b, :].rearrange("p (m t) -> p m t", t=T),
                                       gain_o[:, 0:1], xs[:, 2 * b:2 * b + 2, 0, :].bitcast(F32),
                                       ALU.mult, ALU.subtract).then_inc(ho_in, 1)
            gated_lo(1)
            for s in range(C_OUT + RING, C_UP):
                lo(s)

            def gain_out(n, t):
                if (n, t) == (1, 1):
                    dve.wait_ge(split_used, C_UP)
                else:
                    dve.wait_ge(tile_done, 1 if n == 1 else t + 2)
                m = n // 2 * TT + t
                for b in (1, 0):
                    if b == 0:
                        dve.wait_ge(half_sq, 2 * m + 1)
                    half = slice(D // 2 * b, D // 2 * b + D // 2)
                    V.tensor_tensor(xn2[:, t, half], ps[:, 4 * t + 2 * b:4 * t + 2 * b + 2, :]
                                    .rearrange("p b n -> p (b n)"), gain[:, half], ALU.mult).then_inc(out_gained, 1)
                dve.wait_ge(out_gained, 2 * m + 2)

            def add_out(n, t, cols):
                V.scalar_tensor_tensor(x1[:, t, cols], xn2[:, t, cols], stat[:, n, 2, t:t + 1], x1[:, t, cols],
                                       ALU.mult, ALU.add).then_inc(out_sum, 1)

            def pre_ffn(t, b):
                cols = slice(CH * b, CH * b + CH)
                V.scalar_tensor_tensor(xn2[:, t, cols], x1[:, t, cols], stat[:, 2, 2, t:t + 1], gain_ffn[:, cols],
                                       ALU.mult, ALU.mult).then_inc(xn_ready, 1)

            dve.wait_ge(res_in, 32)
            dve.wait_ge(gain1_in, 16)
            dve.wait_ge(gain_ffn_in, 16)
            gain_out(1, 0)
            rstd(1, 0)
            add_out(1, 0, slice(0, D))
            lo(C_UP)
            dve.wait_ge(out_sum, 1)
            rstd(2, 0)
            for b in range(4):
                pre_ffn(0, b)
            gain_out(1, 1)
            rstd(1, 1)
            for b in range(4):
                add_out(1, 1, slice(CH * b, CH * b + CH))
            take_lo(1, 0, 0)
            take_lo(1, 0, 1)
            dve.wait_ge(sq_done, nth(2, 1))
            V.tensor_reduce(stat[:, 2, 0, 1:2], sq4[:, :], AX.X, ALU.add).then_inc(sq4_sum, 1)
            take_lo(1, 0, 2)
            rstd(2, 1)
            dve.wait_ge(out_sum, 5)
            pre_ffn(1, 0)
            pre_ffn(1, 1)
            take_lo(1, 0, 3)
            take_lo(1, 1, 0)
            pre_ffn(1, 2)
            take_lo(1, 1, 1)
            pre_ffn(1, 3)
            take_lo(1, 1, 2)
            take_lo(1, 1, 3)
            dve.wait_ge(pool_lo, 3)
            dve.sem_inc(lo_ready, 3)

            def lo_loop(j, s):
                dve.wait_ge(hi_ready, s)
                V.tensor_tensor(w_lo[:, j, :], raw[:, j, :], w_hi[:, j, :].bitcast(F32), ALU.subtract)\
                    .then_inc(lo_ready, 1)

            def merge(i, a):
                for b in (0, 1):
                    dve.wait_ge(half_out, i * 4 + (2 * a + b + 1))
                    V.tensor_tensor(pre[a][:, 2 * b:2 * b + 2, :], ps[:, 4 * a + 2 * b:4 * a + 2 * b + 2, 0:T],
                                    pre[a][:, 2 * b:2 * b + 2, :], ALU.add).then_inc(merged, 1)

            def older_taps(i, a):
                for b in (0, 1):
                    dve.wait_ge(ca_ready, i * 4 + (2 * a + b + 1))
                    for tap in (1, 0):
                        back = 2 - tap
                        if tap == 0:
                            dve.wait_ge(taps_done, i * 16 + (8 * a + 4 * b + 3))
                        for m in (2 * b, 2 * b + 1):
                            col = i * 4 + (m + FT * a)
                            V.scalar_tensor_tensor(ca[a][:, m, back:T], pre[a][:, m, 0:T - back],
                                                   conv[:, tap, bass.ds(col, 1)], ca[a][:, m, back:T],
                                                   ALU.mult, ALU.add).then_inc(taps_done, 1)

            dve.sem_inc(taps_done, 1)
            dve.sem_inc(h_ready, 1)
            def hidden_lo(j, k, n):
                dve.wait_ge(hs_hi, n)
                V.tensor_tensor(xs[:, j:j + 1, 1, :], hT[:, k, :], xs[:, j:j + 1, 0, :].bitcast(F32), ALU.subtract)\
                    .then_inc(hs_ready, 1)

            def unit(i, last):
                for j in range(RING):
                    lo_loop(j, i * 8 + (C_UP + RING + j + 1))
                merge(i, 0)
                older_taps(i, 0)
                for j in range(RING):
                    lo_loop(j, i * 8 + (C_UP + 2 * RING + j + 1))
                    if last and j == 0:
                        dve.wait_ge(hs_hi, RING)
                        V.tensor_tensor(xs[:, 0:RING, 1, :], hT[:, 0:RING, :], xs[:, 0:RING, 0, :].bitcast(F32),
                                        ALU.subtract).then_inc(hs_ready, RING)
                merge(i, 1)
                older_taps(i, 1)
                dve.wait_ge(taps_done, i * 16 + 17)
                dve.wait_ge(silu_done, i + 1)
                V.tensor_tensor(hT[:, bass.ds(i * 4, 4), :], ca[0], ca[1], ALU.mult).then_inc(h_ready, 1)

            with dve.Fori(0, UNITS_FFN - 1) as i:
                unit(i, False)
            unit(UNITS_FFN - 1, True)
            with dve.Fori(0, FT // RING - 1) as i:
                for j in range(RING):
                    lo_loop(j, i * RING + (C_DOWN + RING + j + 1))
                    hidden_lo(j, bass.ds(i * RING + (RING + j), 1), i * RING + (RING + j + 1))
            dve.wait_ge(gain2_in, 16)
            gain_out(3, 0)
            rstd(3, 0)
            add_out(3, 0, slice(0, D))
            gain_out(3, 1)
            rstd(3, 1)
            for q in range(4):
                add_out(3, 1, slice(CH * q, CH * q + CH))

        @block.tensor
        def _(pe):
            mm = nc.tensor.matmul

            def turn(n, t, src):
                for b in range(4):
                    pe.wait_ge(xn_ready, t + 1 if n == 0 else TT + 4 * t + b + 1)
                    for kk in range(4):
                        last = nc.tensor.transpose(turned_ps(n, t, b)[:, kk, :],
                                                   src[:, t, P * (4 * b + kk):P * (4 * b + kk) + P], ident[:, :])
                    last.then_inc(turn_done, 1)

            def channels_chunk(j, unit, k0, first, last_chunk, act_k0, kks=range(CK)):
                hi_w, lo_w = grid(w_hi, j), grid(w_lo, j)
                for kk in kks:
                    start, stop = first and kk == 0, last_chunk and kk == CK - 1
                    x_hi, x_lo = xs[:, act_k0 + k0 + kk, 0, :], xs[:, act_k0 + k0 + kk, 1, :]
                    for m in range(4):
                        w = slice(P * m, P * m + P)
                        dst = acc(unit, m)
                        mm(dst, hi_w[:, kk, w], x_hi, start=start and m % 2 == 0, stop=False, skip_group_check=True)
                        mm(dst, hi_w[:, kk, w], x_lo, start=False, stop=False, skip_group_check=True)
                        last = mm(dst, lo_w[:, kk, w], x_hi, start=False, stop=stop, skip_group_check=True)
                return last

            def tokens_tile(j, k, t, start, stop, n_free=None):
                x_hi, x_lo = xs[:, k, 0, P * t:P * t + P], xs[:, k, 1, P * t:P * t + P]
                for stat_op, ring, first, end in ((x_hi, w_hi, True, False), (x_hi, w_lo, False, False),
                                                  (x_lo, w_hi, False, True)):
                    for n in range(4):
                        if first and n == 2 and n_free:
                            n_free()
                        last = mm(ps[:, 4 * t + n, :], stat_op, ring[:, j, CH * n:CH * n + CH],
                                  start=start and first, stop=stop and end)
                return last

            def v_step(n, kk):
                half, quarter = V_ORDER[n]
                j = (C_V + n) % RING
                hi_w, lo_w = grid(w_hi, j)[:, kk, :], grid(w_lo, j)[:, kk, :]
                k = CK * quarter + kk
                start, stop = quarter == 2 and kk == 0, quarter == 1 and kk == CK - 1
                for t in range(TT):
                    x_hi, x_lo = xs[:, k, 0, P * t:P * t + P], xs[:, k, 1, P * t:P * t + P]
                    dst = ps[:, 2 * half + t, :]
                    mm(dst, x_hi, hi_w, start=start, stop=False, skip_group_check=True)
                    mm(dst, x_hi, lo_w, start=False, stop=False, skip_group_check=True)
                    last = mm(dst, x_lo, hi_w, start=False, stop=stop, skip_group_check=True)
                return last

            pe.wait_ge(pool_ready, 5)
            pe.wait_ge(gain0_in, 16)
            nc.tensor.transpose(ps[:, 7, 0:KT], gain_rows[:, :], ident[0:KT, 0:KT]).then_inc(gain0_turned, 1)
            pe.wait_ge(gain0_ready, 1)
            for t in range(TT):
                turn(0, t, x_nat)

            def u_chunk(c):
                pe.wait_ge(xs_ready, taken(0, 1, min(c, 3)))
                pe.wait_ge(lo_ready, c + 1)
                channels_chunk(c % RING, c // 4, CK * (c % 4), c % 4 == 0, c % 4 == 3, 0).then_inc(split_used, 1)

            u_chunk(0)
            u_chunk(1)
            pe.wait_ge(rows_in, 16 * 3)
            pe.wait_ge(rows_ready, 1)
            pe.wait_ge(xs_ready, taken(0, 0, 2))
            nc.tensor.transpose(ps[:, 4, 0:3 * NT], rows[0:3 * NT, :], ident[0:3 * NT, 0:3 * NT])\
                .then_inc(prep_done, 1)
            u_chunk(2)
            pe.wait_ge(xs_ready, taken(0, 1, 3))
            pe.wait_ge(rows2_in, 32)
            nc.tensor.transpose(ps[:, 5, 0:UT + 1], rows2[0:UT + 1, :], ident[0:UT + 1, 0:UT + 1])\
                .then_inc(prep_done, 1)
            pe.wait_ge(conv_in, 32)
            for n in range(4):
                last = nc.tensor.transpose(ps[:, 6, 2 * FT * n:2 * FT * n + 2 * FT], rows_conv[0:2 * FT, n, :],
                                           ident[0:2 * FT, 0:2 * FT])
            last.then_inc(prep_done, 1)
            pe.wait_ge(pool_ready, 11)
            pe.wait_ge(rel_in, 32)
            mm(ps[0:HEADS, 7, 0:BAND], relb, onehot, start=True, stop=True).then_inc(prep_done, 1)
            u_chunk(3)
            pe.wait_ge(c_in, 64)
            for n in range(4, 8):
                a, q = divmod(n - 4, 2)
                pe.wait_ge(prep_out, n - 3)
                for j in range(4):
                    last = nc.tensor.transpose(ps[:, 4 + n % 4, P * j:P * j + P],
                                               c_nat[a][:, 4 * q + j, :, :].rearrange("p e q -> p (e q)"), ident[:, :])
                last.then_inc(prep_done, 1)
            for c in (4, 5):
                u_chunk(c)
            pe.wait_ge(lam_v, 4)
            pe.wait_ge(prep_out, 5)
            mm(ps[:, 4, 0:1], ones[:, :], lams[:, 5:6], start=True, stop=True).then_inc(prep_done, 1)

            def turn_b(n0, diag):
                for n in range(n0, n0 + 4):
                    a, q = divmod(n - n0, 2)
                    pe.wait_ge(prep_out, n - 3)
                    for j in range(4):
                        jj = 4 * q + j
                        last = nc.tensor.transpose(ps[:, 4 + n % 4, P * j:P * j + P],
                                                   diag[a][:, 4 * jj:4 * jj + 4, :, :]
                                                   .rearrange("p i e h -> p (i e h)"), ident[:, :])
                    last.then_inc(prep_done, 1)

            pe.wait_ge(bdiag_ready, 4)
            turn_b(9, b_diag)
            pe.wait_ge(prep_out, 10)
            for q in range(4):
                for j in range(UT):
                    for a in (0, 1):
                        last = mm(ps[32 * q:32 * q + 32, 5, 32 * j:32 * j + 32],
                                  b_diag[a][:, 4 * j + q, :, :].rearrange("p e h -> p (e h)"),
                                  CS[a][:, 4 * j + q, :, :].rearrange("p e h -> p (e h)"),
                                  start=j == 0 and a == 0, stop=a == 1, skip_group_check=True)
            last.then_inc(prep_done, 1)
            u_chunk(6)
            pe.wait_ge(bdiag2_ready, 4)
            turn_b(14, b_diag2)
            u_chunk(7)

            def state_rows(i):
                return slice(32 * (i % 4), 32 * (i % 4) + 32), i // 4

            def b_u(p):
                if p >= 2:
                    pe.wait_ge(bu_used, p - 1)
                if p == PAIRS // 2:
                    pe.wait_ge(acc_out, 2)
                for e in (0, 1):
                    rows_i, j = state_rows(tile_of(p, e))
                    u = uT[rows_i, j, :].rearrange("p (m o) -> p o m", o=2)
                    for a in (0, 1):
                        dst = ps[:, 4 + p % 2, 2 * M * a + M * e:2 * M * a + M * e + M]
                        mm(dst, BT2[a][rows_i, j, :], u[:, 0, :], start=e == 0 and a == 0, stop=False,
                           skip_group_check=True)
                        last = mm(dst, BT[a][rows_i, j, :], u[:, 1, :], start=False, stop=True, skip_group_check=True)
                last.then_inc(bu_done, 1)

            def c_x(p):
                group, q = divmod(p, 4)
                pe.wait_ge(state_ready, 2 * p + 2)
                if q == 0 and group >= 2:
                    pe.wait_ge(y_out, 2 * group - 2)
                for e in (0, 1):
                    i = tile_of(p, e)
                    rows_i, j = state_rows(i)
                    y = ps[rows_i, 6 + group % 2, T * e:T * e + T]
                    u = uT[rows_i, j, :].rearrange("p (m o) -> p o m", o=2)
                    mm(y[:, 0:M], K0T[rows_i, j, :], u[:, 0, :], start=e == 0, stop=False, skip_group_check=True)
                    for a in (0, 1):
                        mm(y[:, 0:M], CS2[a][:, i, :], state[p % 2][:, a, e, 0:M], start=False, stop=a == 1,
                           skip_group_check=True)
                    for a in (0, 1):
                        last = mm(y[:, M:T], CS[a][:, i, :, :].rearrange("p e h -> p (e h)"),
                                  state[p % 2][:, a, e, 1:M + 1], start=False, stop=a == 1, skip_group_check=True)
                last.then_inc(y_done, 1)

            pe.wait_ge(acc_out, 1)
            pe.wait_ge(prep_out, 18)

            def qkv_chunk(c, s0):
                pe.wait_ge(lo_ready, c + 1)
                if c < C_V:
                    unit, quarter = divmod(c - C_QK, 4)
                    if quarter == 0:
                        pe.wait_ge(acc_out, unit + 1)
                elif c - C_V in (0, 2):
                    pe.wait_ge(acc_out, 5 + (c - C_V) // 2)
                for kk in range(CK):
                    p = (s0 + kk) // SSM_STEP
                    if (s0 + kk) % SSM_STEP == 0 and p < PAIRS + 2:
                        if p < PAIRS:
                            b_u(p)
                        if p == 2:
                            pe.wait_ge(cs2_ready[0], 1)
                            pe.wait_ge(cs2_ready[1], 1)
                        if p >= 2:
                            c_x(p - 2)
                    if c < C_V:
                        last = channels_chunk(c % RING, unit, CK * quarter, quarter == 0, quarter == 3, 0, (kk,))
                    else:
                        last = v_step(c - C_V, kk)
                last.then_inc(split_used, 1)

            for c in range(C_QK, C_V + 6):
                qkv_chunk(c, CK * (c - C_QK))

            def scores(h):
                if h == 0:
                    pe.wait_ge(acc_out, 6)
                    pe.wait_ge(bu_used, PAIRS)
                else:
                    pe.wait_ge(sc_read, 2 * h)
                for s in (0, 1):
                    half = slice(DH * s, DH * s + DH)
                    mm(ps[:, 4 + s, 0:P], qT[half, h, 0:P], kT[half, h, 0:P], start=True, stop=True)
                    last = mm(ps[:, 4 + s, P:P + T], qT[half, h, P:T], kT[half, h, :], start=True, stop=True)
                last.then_inc(sc_done, 1)

            def turn_att(h):
                pe.wait_ge(att_ready, 2 * h + 2)
                if h >= 1:
                    pe.wait_ge(attT_ready, h)
                for b in range(3):
                    last = nc.tensor.transpose(ps[:, 6, P * b:P * b + P], att[h % 2][:, P * b:P * b + P], ident[:, :])
                last.then_inc(att_turned, 1)

            def att_v(h):
                pe.wait_ge(attT_ready, h + 1)
                pe.wait_ge(acc_out, 8)
                if h >= 1:
                    pe.wait_ge(hs_std, TT * h)
                cols = slice(P * h, P * h + P)
                mm(ps[:, 7, 0:P], attT[h % 2][:, 0:P], v[:, 0, cols], start=True, stop=True)
                mm(ps[:, 7, P:T], attT[h % 2][:, P:T], v[:, 0, cols], start=True, stop=False)
                mm(ps[:, 7, P:T], attT[h % 2][:, T:T + P], v[:, 1, cols], start=False, stop=True)\
                    .then_inc(av_done, 1)

            scores(0)
            for c in range(C_V + 6, C_GLU):
                qkv_chunk(c, CK * (c - C_QK))
            pe.wait_ge(y_out, UT)
            pe.wait_ge(acc_out, 7)
            pe.wait_ge(glu_in, 1)
            for c in range(HEADS):
                if c + 1 < HEADS:
                    scores(c + 1)
                turn_att(c)
                unit, half = divmod(c, 2)
                if half == 0 and unit >= 2:
                    pe.wait_ge(acc_out, 8 + unit - 1)
                pe.wait_ge(lo_ready, C_GLU + c + 1)
                channels_chunk((C_GLU + c) % RING, unit, CK * half, half == 0, half == 1, UT).then_inc(split_used, 1)
                att_v(c)

            def out_tile(n, t, n_free=None):
                return tokens_tile((C_OUT + n) % RING, OUT_ORDER[n], t, n == 0, n == KT - 1, n_free)

            pe.wait_ge(z_in, 1)
            pe.wait_ge(acc_out, 11)
            for n in range(RING):
                pe.wait_ge(lo_ready, C_OUT + n + 1)
                if n == RING - 1:
                    pe.wait_ge(ho_ready, 1)
                    for b in range(4):
                        for m in range(2):
                            for t in range(TT):
                                last = nc.tensor.transpose(ps[:, 4 + b, T * m + P * t:T * m + P * t + P],
                                                           heads_out[:, TT * (2 * b + m) + t, :], ident[:, :])
                        last.then_inc(ho_turned, 1)
                out_tile(n, 0, (lambda: pe.wait_ge(acc_out, 12)) if n == 0 else None)
            pe.wait_ge(ho_in, 4)
            for n in range(RING):
                out_tile(n, 1).then_inc(split_used, 1)
            pe.wait_ge(z_in, 2)
            for n in range(RING, KT - RING):
                pe.wait_ge(lo_ready, C_OUT + n + 1)
                out_tile(n, 0)
                out_tile(n, 1).then_inc(split_used, 1)
            for n in range(KT - RING, KT):
                pe.wait_ge(lo_ready, C_OUT + n + 1)
                last = out_tile(n, 0)
            last.then_inc(tile_done, 1)
            for n in range(KT - RING, KT):
                out_tile(n, 1).then_inc(split_used, 1)

            for t in range(TT):
                turn(1, t, xn2)
            def up_chunk(q, half):
                hi_w, lo_w = grid(w_hi, q), grid(w_lo, q)
                for kk in range(CK):
                    k, start, stop = CK * q + kk, q == 0 and kk == 0, q == 3 and kk == CK - 1
                    for m in range(4):
                        w = slice(P * m, P * m + P)
                        mm(ps[:, 4 * half + m, :], hi_w[:, kk, w], xs[:, k, :, :].rearrange("p e t -> p (e t)"),
                           start=start, stop=False, skip_group_check=True)
                        last = mm(ps[:, 4 * half + m, 0:T], lo_w[:, kk, w], xs[:, k, 0, :], start=False, stop=stop,
                                  skip_group_check=True)
                last.then_inc(split_used, 1)

            for q in range(4):
                pe.wait_ge(xs_ready, turned(1, 1, q))
                if q == 0:
                    pe.wait_ge(lo_ready, C_UP + 1)
                else:
                    pe.wait_ge(pool_lo, q)
                up_chunk(q, 0)
            for q in range(4):
                pe.wait_ge(lo_ready, C_UP + 4 + q + 1)
                up_chunk(q, 1)
            with pe.Fori(1, UNITS_FFN) as i:
                for half in (0, 1):
                    pe.wait_ge(merged, i * 4 + (2 * half - 2))
                    for q in range(4):
                        pe.wait_ge(lo_ready, i * 8 + (C_UP + 4 * half + q + 1))
                        up_chunk(q, half)

            def down_ready(i, j):
                pe.wait_ge(hs_ready, i * RING + (j + 1))
                pe.wait_ge(lo_ready, i * RING + (C_DOWN + j + 1))

            for j in range(RING):
                down_ready(0, j)
                if j == 0:
                    pe.wait_ge(merged, 4 * UNITS_FFN - 2)
                tokens_tile(j, j, 0, j == 0, False)
            pe.wait_ge(merged, 4 * UNITS_FFN)
            for j in range(RING):
                tokens_tile(j, j, 1, j == 0, False).then_inc(split_used, 1)
            with pe.Fori(1, FT // RING - 1) as i:
                for j in range(RING):
                    down_ready(i, j)
                    for t in range(TT):
                        last = tokens_tile(j, j, t, False, False)
                    last.then_inc(split_used, 1)
            for t in range(TT):
                for j in range(RING):
                    if t == 0:
                        down_ready(FT // RING - 1, j)
                    last = tokens_tile(j, j, t, False, j == RING - 1)
                last.then_inc(tile_done, 1)


_INS = ['x', 'ln_pre_mix', 'ln_post_mix', 'ln_pre_ffn', 'ln_post_ffn', 'w_in', 'lam_q1', 'lam_k1', 'lam_q2', 'lam_k2',
        'attn_sub_norm', 'rel_bias', 'ssm_a_re', 'ssm_a_im', 'ssm_log_dt', 'ssm_b_re', 'ssm_b_im', 'ssm_c_re',
        'ssm_c_im', 'ssm_d', 'ssm_w_glu', 'w_out', 'w_up', 'conv_w', 'conv_b', 'w_down']


def _bucket_onehot():
    import numpy as np
    table = np.zeros((NB + 1, BAND), np.float32)
    for m in range(BAND):
        dist = T - 1 - m
        if dist < 0:
            b = NB
        elif dist < NB // 2:
            b = dist
        else:
            b = min(NB - 1, NB // 2 + int(math.log(dist / 16) / math.log(128 / 16) * (NB // 2)))
        table[b, m] = 1.0
    return table


def kernel(**inputs):
    import numpy as _np
    import concourse.bacc as _bacc
    from concourse import mybir as _mybir
    from concourse.bass_utils import run_bass_kernel_spmd as _run

    nc = _bacc.Bacc("TRN2", target_bir_lowering=False, num_devices=1, dynamic_dma_scratch_size=1024)
    arrays, args = {}, []
    given = {name: _np.ascontiguousarray(inputs[name]) for name in _INS}
    given["bucket_onehot"] = _bucket_onehot()
    for name, a in given.items():
        arrays[f"in_{name}_dram"] = a
        args.append(nc.dram_tensor(f"in_{name}_dram", a.shape, _mybir.dt.from_np(a.dtype), kind="ExternalInput").ap())
    args.append(nc.dram_tensor("out_0_dram", (1, T, D), F32, kind="ExternalOutput").ap())
    build(nc, *args)
    r = _run(nc, [arrays], core_ids=[0])
    return r.results[0]["out_0_dram"]
```
